# Optimizing a Trainium2 kernel written in Bass

```python
import jax, jax.numpy as jnp
from jax import lax
import numpy as np

D_MODEL = 1024
BATCH = 1
SEQ = 512
DEPTH = 1

CHUNK = 64
POOL_GROUPS = 4
POOL_WINDOWS = (2, 4, 8, 16)
POOL_WIDTH = D_MODEL // 2
POOL_GROUP_DIM = POOL_WIDTH // POOL_GROUPS
SB_HEAD_DIM = 64
SB_HEADS = D_MODEL // 128
SB_WIDTH = SB_HEADS * SB_HEAD_DIM
SB_BLOCK = 128
MEM_LEN = 256
X_HEADS = 4
X_HEAD_DIM = D_MODEL // 16
X_WIDTH = X_HEADS * X_HEAD_DIM
N_BRANCHES = 3
D_FF = -(-8 * D_MODEL // (3 * 256)) * 256
RMS_EPS = 1e-6
IN_WIDTH = POOL_WIDTH + 3 * SB_WIDTH + X_WIDTH + N_BRANCHES * D_MODEL


def rmsnorm(x, g):
    xf = x.astype(jnp.float32)
    y = xf * lax.rsqrt(jnp.mean(xf * xf, axis=-1, keepdims=True) + RMS_EPS) * g.astype(jnp.float32)
    return y.astype(x.dtype)

def pool_mixer(p, w_mix, scale):
    b, s, _ = p.shape
    pg = p.astype(jnp.float32).reshape(b, s, POOL_GROUPS, POOL_GROUP_DIM)
    c = jnp.concatenate([jnp.zeros((b, 1, POOL_GROUPS, POOL_GROUP_DIM), jnp.float32),
                         jnp.cumsum(pg, axis=1)], axis=1)
    windows = jnp.array(POOL_WINDOWS, jnp.int32)
    t1 = jnp.arange(1, s + 1, dtype=jnp.int32)[:, None]
    lo = jnp.maximum(t1 - windows[None, :], 0)
    g_idx = jnp.arange(POOL_GROUPS, dtype=jnp.int32)[None, :]
    c_lo = c[:, lo, g_idx]
    count = jnp.minimum(t1, windows[None, :]).astype(jnp.float32)
    mixed = (c[:, 1:] - c_lo) / count[None, :, :, None] - pg
    mixed = mixed.astype(p.dtype)
    y = jnp.einsum('bsgc,gcd->bsgd', mixed, w_mix)
    return y.reshape(b, s, POOL_WIDTH) * scale

def stick_breaking_attention(q, k, v):
    b, s, h, dh = q.shape
    nb = s // SB_BLOCK
    scale = 1.0 / float(np.sqrt(dh))
    kf = k.astype(jnp.float32).transpose(0, 2, 1, 3)
    vf = v.astype(jnp.float32).transpose(0, 2, 1, 3)
    qb = q.astype(jnp.float32).transpose(0, 2, 1, 3).reshape(b, h, nb, SB_BLOCK, dh)
    qb = qb.transpose(2, 0, 1, 3, 4)
    key_pos = jnp.arange(s, dtype=jnp.int32)[None, :]

    def one_block(args):
        q_blk, bi = args
        z = jnp.einsum('bhqd,bhkd->bhqk', q_blk, kf) * scale
        qpos = bi * SB_BLOCK + jnp.arange(SB_BLOCK, dtype=jnp.int32)[:, None]
        mask = key_pos < qpos
        log1m = jnp.where(mask, jax.nn.log_sigmoid(-z), 0.0)
        excl = lax.cumsum(log1m, axis=3, reverse=True) - log1m
        a = jnp.where(mask, jnp.exp(jax.nn.log_sigmoid(z) + excl), 0.0)
        return jnp.einsum('bhqk,bhkd->bhqd', a, vf)

    out = lax.map(one_block, (qb, jnp.arange(nb, dtype=jnp.int32)))
    out = out.transpose(1, 0, 3, 2, 4).reshape(b, s, h * dh)
    return out.astype(q.dtype)

def memory_cross_attention(q, mem_n, w_mem_kv):
    b, s = q.shape[:2]
    m = mem_n.shape[1]
    kv = (mem_n @ w_mem_kv).reshape(b, m, 2, X_HEADS, X_HEAD_DIM)
    mk, mv = kv[:, :, 0], kv[:, :, 1]
    scores = jnp.einsum('bshd,bmhd->bhsm', q.astype(jnp.float32), mk.astype(jnp.float32))
    p = jax.nn.softmax(scores / float(np.sqrt(X_HEAD_DIM)), axis=-1)
    out = jnp.einsum('bhsm,bmhd->bshd', p, mv.astype(jnp.float32))
    return out.reshape(b, s, X_WIDTH).astype(q.dtype)

def first_inputs(seed: int = 0) -> dict:
    key = jax.random.key(seed)
    ks = jax.random.split(key, 20)
    f32 = jnp.float32

    def nrm(k, shape, fan_in):
        return jax.random.normal(k, shape, f32) * (fan_in ** -0.5)

    def gain(k, shape):
        return 1.0 + 0.02 * jax.random.normal(k, shape, f32)

    L = DEPTH
    return {
        "x": jax.random.normal(ks[0], (BATCH, SEQ, D_MODEL), f32),
        "mem": jax.random.normal(ks[1], (BATCH, MEM_LEN, D_MODEL), f32),
        "norm_mix_pre": gain(ks[2], (L, D_MODEL)),
        "w_in": nrm(ks[3], (L, D_MODEL, IN_WIDTH), D_MODEL),
        "w_pool_mix": nrm(ks[4], (L, POOL_GROUPS, POOL_GROUP_DIM, POOL_GROUP_DIM), POOL_GROUP_DIM),
        "pool_scale": gain(ks[5], (L, POOL_WIDTH)),
        "w_pool_o": nrm(ks[6], (L, POOL_WIDTH, D_MODEL), POOL_WIDTH),
        "w_sb_o": nrm(ks[7], (L, SB_WIDTH, D_MODEL), SB_WIDTH),
        "norm_mem": gain(ks[8], (L, D_MODEL)),
        "w_mem_kv": nrm(ks[9], (L, D_MODEL, 2 * X_WIDTH), D_MODEL),
        "w_x_o": nrm(ks[10], (L, X_WIDTH, D_MODEL), X_WIDTH),
        "w_out": nrm(ks[11], (L, D_MODEL, D_MODEL), D_MODEL),
        "norm_mix_post": gain(ks[12], (L, D_MODEL)),
        "norm_ffn_pre": gain(ks[13], (L, D_MODEL)),
        "w_ffn_in": nrm(ks[14], (L, D_MODEL, 2 * D_FF), D_MODEL),
        "w_ffn_out": nrm(ks[15], (L, D_FF, D_MODEL), D_FF),
        "norm_ffn_post": gain(ks[16], (L, D_MODEL)),
    }

def first_block(x, mem, norm_mix_pre, w_in, w_pool_mix, pool_scale, w_pool_o, w_sb_o,
              norm_mem, w_mem_kv, w_x_o, w_out, norm_mix_post, norm_ffn_pre,
              w_ffn_in, w_ffn_out, norm_ffn_post):
    b, s, d = x.shape
    h = x
    for l in range(DEPTH):
        n = rmsnorm(h, norm_mix_pre[l])
        proj = n @ w_in[l]
        o0 = POOL_WIDTH
        o1 = o0 + 3 * SB_WIDTH
        o2 = o1 + X_WIDTH
        p_in = proj[..., :o0]
        qkv = proj[..., o0:o1].reshape(b, s, 3, SB_HEADS, SB_HEAD_DIM)
        xq = proj[..., o1:o2].reshape(b, s, X_HEADS, X_HEAD_DIM)
        gates = jax.nn.sigmoid(proj[..., o2:].astype(jnp.float32)).reshape(b, s, N_BRANCHES, d)

        y_pool = pool_mixer(p_in, w_pool_mix[l], pool_scale[l]) @ w_pool_o[l]
        y_sb = stick_breaking_attention(qkv[:, :, 0], qkv[:, :, 1], qkv[:, :, 2]) @ w_sb_o[l]
        mem_n = rmsnorm(mem, norm_mem[l])
        y_x = memory_cross_attention(xq, mem_n, w_mem_kv[l]) @ w_x_o[l]

        merged = (gates[:, :, 0] * y_pool.astype(jnp.float32)
                  + gates[:, :, 1] * y_sb.astype(jnp.float32)
                  + gates[:, :, 2] * y_x.astype(jnp.float32)).astype(h.dtype)
        h = h + rmsnorm(merged @ w_out[l], norm_mix_post[l])

        n2 = rmsnorm(h, norm_ffn_pre[l])
        gu = n2 @ w_ffn_in[l]
        ff = (jax.nn.silu(gu[..., :D_FF]) * gu[..., D_FF:]) @ w_ffn_out[l]
        h = h + rmsnorm(ff, norm_ffn_post[l])
    return h


DEPTH_2 = 2

N_MIXERS = 2
N_HGRN_LAYERS = (DEPTH_2 + 1) // 2
N_MLA_LAYERS = DEPTH_2 // 2

HGRN_EXPAND = 128
HGRN_HEADS = D_MODEL // HGRN_EXPAND
HGRN_VDIM = D_MODEL // HGRN_HEADS
HGRN_CHUNK = 64

MLA_HEADS = D_MODEL // 128
MLA_NOPE = 128
MLA_ROPE = 64
MLA_QK_HEAD = MLA_NOPE + MLA_ROPE
MLA_V_HEAD = 128
MLA_Q_LORA = D_MODEL // 4
MLA_KV_LORA = D_MODEL // 4
ROPE_THETA = 10000.0
Q_BLOCK = 128

D_FF_2 = 2816
FFN_CONV = 3


def _rmsnorm(x, gain):
    xf = x.astype(jnp.float32)
    y = xf * lax.rsqrt(jnp.mean(xf * xf, axis=-1, keepdims=True) + RMS_EPS)
    return (y * gain.astype(jnp.float32)).astype(x.dtype)

def _chunk_gated_recurrence(q, k, v, log_f):
    B, S, H, Dk = q.shape
    Dv = v.shape[-1]
    C = HGRN_CHUNK
    N = S // C

    def to_chunks(t):
        return t.astype(jnp.float32).reshape(B, N, C, H, t.shape[-1]).transpose(1, 0, 3, 2, 4)

    causal = jnp.tril(jnp.ones((C, C), dtype=bool))[:, :, None]

    def step(state, inp):
        qc, kc, vc, gc = inp
        G = jnp.cumsum(gc, axis=2)
        o_inter = jnp.einsum("bhtd,bhde->bhte", qc * jnp.exp(G), state)
        diff = G[:, :, :, None, :] - G[:, :, None, :, :]
        decay = jnp.where(causal, jnp.exp(jnp.where(causal, diff, 0.0)), 0.0)
        scores = jnp.einsum("bhtd,bhsd,bhtsd->bhts", qc, kc, decay)
        o_intra = jnp.einsum("bhts,bhse->bhte", scores, vc)
        G_last = G[:, :, -1:, :]
        new_state = state * jnp.exp(G_last[:, :, 0, :, None]) + jnp.einsum(
            "bhsd,bhse->bhde", kc * jnp.exp(G_last - G), vc)
        return new_state, o_inter + o_intra

    state0 = jnp.zeros((B, H, Dk, Dv), jnp.float32)
    _, o = lax.scan(step, state0, (to_chunks(q), to_chunks(k), to_chunks(v), to_chunks(log_f)))
    return o.transpose(1, 0, 3, 2, 4).reshape(B, S, H, Dv)

def _hgrn2_mixer(h, w_in, lower_bound, out_norm, w_out):
    B, S, _ = h.shape
    q, f, i, g = jnp.split(h @ w_in, 4, axis=-1)

    def heads(t):
        return t.reshape(B, S, HGRN_HEADS, -1)

    lb = lower_bound.astype(jnp.float32)
    forget = lb + (1.0 - lb) * jax.nn.sigmoid(f.astype(jnp.float32))
    key_in = 1.0 - forget
    log_f = jnp.log(forget)
    o = _chunk_gated_recurrence(heads(jax.nn.silu(q)), heads(key_in), heads(i), heads(log_f))
    o = _rmsnorm(o, out_norm) * jax.nn.silu(heads(g.astype(jnp.float32)))
    return o.reshape(B, S, D_MODEL).astype(h.dtype) @ w_out

def _rope_tail(x, cos, sin):
    x_nope, x1, x2 = jnp.split(x, [MLA_NOPE, MLA_NOPE + MLA_ROPE // 2], axis=-1)
    xf1 = x1.astype(jnp.float32)
    xf2 = x2.astype(jnp.float32)
    rot = jnp.concatenate([xf1 * cos - xf2 * sin, xf2 * cos + xf1 * sin], axis=-1).astype(x.dtype)
    return jnp.concatenate([x_nope, rot], axis=-1)

def _causal_block_attention(q, k, v):
    B, S, H, Dqk = q.shape
    nb = S // Q_BLOCK
    scale = Dqk ** -0.5
    q_blocks = q.reshape(B, nb, Q_BLOCK, H, Dqk).transpose(1, 0, 3, 2, 4)
    k_t = k.transpose(0, 2, 1, 3)
    v_t = v.transpose(0, 2, 1, 3)
    key_pos = jnp.arange(S)

    def attend(args):
        q_blk, blk = args
        s = jnp.einsum("bhqd,bhkd->bhqk", q_blk, k_t).astype(jnp.float32) * scale
        q_pos = blk * Q_BLOCK + jnp.arange(Q_BLOCK)
        s = jnp.where(key_pos[None, :] <= q_pos[:, None], s, -jnp.inf)
        p = jax.nn.softmax(s, axis=-1).astype(v_t.dtype)
        return jnp.einsum("bhqk,bhkv->bhqv", p, v_t)

    o = lax.map(attend, (q_blocks, jnp.arange(nb)))
    return o.transpose(1, 0, 3, 2, 4).reshape(B, S, H, -1)

def _mla_mixer(h, cos, sin, w_in, q_a_norm, w_q_up, kv_a_norm, w_kv_up, q_norm, k_norm, w_out):
    B, S, _ = h.shape
    c_q, c_kv, k_rope = jnp.split(h @ w_in, [MLA_Q_LORA, MLA_Q_LORA + MLA_KV_LORA], axis=-1)
    q = (_rmsnorm(c_q, q_a_norm) @ w_q_up).reshape(B, S, MLA_HEADS, MLA_QK_HEAD)
    kv = (_rmsnorm(c_kv, kv_a_norm) @ w_kv_up).reshape(B, S, MLA_HEADS, MLA_NOPE + MLA_V_HEAD)
    k_nope, v = jnp.split(kv, [MLA_NOPE], axis=-1)
    k = jnp.concatenate(
        [k_nope, jnp.broadcast_to(k_rope[:, :, None, :], (B, S, MLA_HEADS, MLA_ROPE))], axis=-1)
    q = _rope_tail(_rmsnorm(q, q_norm), cos, sin)
    k = _rope_tail(_rmsnorm(k, k_norm), cos, sin)
    o = _causal_block_attention(q, k, v)
    return o.reshape(B, S, MLA_HEADS * MLA_V_HEAD) @ w_out

def _conv_ffn(h, w_up, conv_w, conv_b, w_down):
    S = h.shape[1]
    u = h @ w_up
    u_pad = jnp.pad(u, ((0, 0), (FFN_CONV - 1, 0), (0, 0)))
    y = conv_b.astype(u.dtype)
    for j in range(FFN_CONV):
        y = y + u_pad[:, j:j + S, :] * conv_w[j]
    gate, up = jnp.split(y, 2, axis=-1)
    return (jax.nn.silu(gate) * up) @ w_down

def second_inputs(seed: int = 0) -> dict:
    key = jax.random.key(seed)
    ks = iter(jax.random.split(key, 32))

    def nrm(shape, scale):
        return jax.random.normal(next(ks), shape, jnp.float32) * scale

    def gain(shape):
        return 1.0 + 0.02 * jax.random.normal(next(ks), shape, jnp.float32)

    D = D_MODEL
    x = jax.random.normal(next(ks), (BATCH, SEQ, D), jnp.float32)
    offsets = jax.random.randint(next(ks), (BATCH, 1), 0, 4096, dtype=jnp.int32)
    positions = offsets + jnp.arange(SEQ, dtype=jnp.int32)[None, :]
    return {
        "x": x,
        "positions": positions,
        "norm_mix": gain((DEPTH_2, D)),
        "norm_ffn": gain((DEPTH_2, D)),
        "hgrn_w_in": nrm((N_HGRN_LAYERS, D, 4 * D), D ** -0.5),
        "hgrn_lower_bounds": nrm((N_HGRN_LAYERS, HGRN_HEADS * HGRN_EXPAND), 0.1),
        "hgrn_out_norm": gain((N_HGRN_LAYERS, HGRN_VDIM)),
        "hgrn_w_out": nrm((N_HGRN_LAYERS, D, D), D ** -0.5),
        "mla_w_in": nrm((N_MLA_LAYERS, D, MLA_Q_LORA + MLA_KV_LORA + MLA_ROPE), D ** -0.5),
        "mla_q_a_norm": gain((N_MLA_LAYERS, MLA_Q_LORA)),
        "mla_w_q_up": nrm((N_MLA_LAYERS, MLA_Q_LORA, MLA_HEADS * MLA_QK_HEAD), MLA_Q_LORA ** -0.5),
        "mla_kv_a_norm": gain((N_MLA_LAYERS, MLA_KV_LORA)),
        "mla_w_kv_up": nrm((N_MLA_LAYERS, MLA_KV_LORA, MLA_HEADS * (MLA_NOPE + MLA_V_HEAD)), MLA_KV_LORA ** -0.5),
        "mla_q_norm": gain((N_MLA_LAYERS, MLA_QK_HEAD)),
        "mla_k_norm": gain((N_MLA_LAYERS, MLA_QK_HEAD)),
        "mla_w_out": nrm((N_MLA_LAYERS, MLA_HEADS * MLA_V_HEAD, D), (MLA_HEADS * MLA_V_HEAD) ** -0.5),
        "ffn_w_up": nrm((DEPTH_2, D, 2 * D_FF_2), D ** -0.5),
        "ffn_conv_w": nrm((DEPTH_2, FFN_CONV, 2 * D_FF_2), FFN_CONV ** -0.5),
        "ffn_conv_b": nrm((DEPTH_2, 2 * D_FF_2), 0.01),
        "ffn_w_down": nrm((DEPTH_2, D_FF_2, D), D_FF_2 ** -0.5),
    }

def second_block(x, positions, norm_mix, norm_ffn, hgrn_w_in, hgrn_lower_bounds, hgrn_out_norm, hgrn_w_out,
              mla_w_in, mla_q_a_norm, mla_w_q_up, mla_kv_a_norm, mla_w_kv_up, mla_q_norm, mla_k_norm,
              mla_w_out, ffn_w_up, ffn_conv_w, ffn_conv_b, ffn_w_down):
    lb_soft = jax.nn.softmax(hgrn_lower_bounds.astype(jnp.float32), axis=0)
    lower_bounds = jnp.cumsum(lb_soft, axis=0) - lb_soft[0:1]
    inv_freq = ROPE_THETA ** (-jnp.arange(0, MLA_ROPE, 2, dtype=jnp.float32) / MLA_ROPE)
    ang = positions.astype(jnp.float32)[..., None] * inv_freq
    cos = jnp.cos(ang)[:, :, None, :]
    sin = jnp.sin(ang)[:, :, None, :]

    for layer in range(DEPTH_2):
        h = _rmsnorm(x, norm_mix[layer])
        j = layer // N_MIXERS
        if layer % N_MIXERS == 0:
            y = _hgrn2_mixer(h, hgrn_w_in[j], lower_bounds[j], hgrn_out_norm[j], hgrn_w_out[j])
        else:
            y = _mla_mixer(h, cos, sin, mla_w_in[j], mla_q_a_norm[j], mla_w_q_up[j], mla_kv_a_norm[j],
                           mla_w_kv_up[j], mla_q_norm[j], mla_k_norm[j], mla_w_out[j])
        x = x + y
        h = _rmsnorm(x, norm_ffn[layer])
        x = x + _conv_ffn(h, ffn_w_up[layer], ffn_conv_w[layer], ffn_conv_b[layer], ffn_w_down[layer])
    return x


def setup_inputs(seed=0):
    out = dict(first_inputs(seed))
    for name, value in second_inputs(seed + 1).items():
        if name != "x":
            out[name + "_2"] = value
    return out


def reference(
    x, mem, norm_mix_pre, w_in, w_pool_mix, pool_scale, w_pool_o, w_sb_o, norm_mem, w_mem_kv,
    w_x_o, w_out, norm_mix_post, norm_ffn_pre, w_ffn_in, w_ffn_out, norm_ffn_post, positions_2,
    norm_mix_2, norm_ffn_2, hgrn_w_in_2, hgrn_lower_bounds_2, hgrn_out_norm_2, hgrn_w_out_2,
    mla_w_in_2, mla_q_a_norm_2, mla_w_q_up_2, mla_kv_a_norm_2, mla_w_kv_up_2, mla_q_norm_2,
    mla_k_norm_2, mla_w_out_2, ffn_w_up_2, ffn_conv_w_2, ffn_conv_b_2, ffn_w_down_2,
):
    x = first_block(
        x, mem, norm_mix_pre, w_in, w_pool_mix, pool_scale, w_pool_o, w_sb_o, norm_mem,
        w_mem_kv, w_x_o, w_out, norm_mix_post, norm_ffn_pre, w_ffn_in, w_ffn_out, norm_ffn_post,
    )
    return second_block(
        x, positions_2, norm_mix_2, norm_ffn_2, hgrn_w_in_2, hgrn_lower_bounds_2,
        hgrn_out_norm_2, hgrn_w_out_2, mla_w_in_2, mla_q_a_norm_2, mla_w_q_up_2,
        mla_kv_a_norm_2, mla_w_kv_up_2, mla_q_norm_2, mla_k_norm_2, mla_w_out_2, ffn_w_up_2,
        ffn_conv_w_2, ffn_conv_b_2, ffn_w_down_2,
    )


_drawn_inputs = setup_inputs


def setup_inputs(seed=0):
    import zlib

    import numpy as np

    out = dict(_drawn_inputs(seed))
    spreads = {}
    factors = {'pool_scale': 3.601,
     'norm_mem': 8.0,
     'norm_mix_post': 3.002,
     'norm_ffn_pre': 2.834,
     'norm_ffn_post': 4.221,
     'norm_mix_2': 5.392,
     'norm_ffn_2': 4.335,
     'hgrn_out_norm_2': 7.423,
     'mla_q_a_norm_2': 8.0,
     'mla_kv_a_norm_2': 8.0,
     'mla_q_norm_2': 8.0,
     'mla_k_norm_2': 8.0,
     'ffn_conv_b_2': 8.0}
    for name, (base, spread) in spreads.items():
        noise = np.random.default_rng([zlib.crc32(name.encode()), seed]).standard_normal(out[name].shape)
        drawn = base * np.exp(spread * noise) if base else spread * noise
        out[name] = __import__('jax').numpy.asarray(drawn.astype(out[name].dtype))
    for name, factor in factors.items():
        out[name] = (out[name] * factor).astype(out[name].dtype)
    return out
```

```python
from contextlib import ExitStack

import numpy as np

import concourse.bass as bass
from concourse import mybir

P = 128
S = 512
D = 1024
KD = D // P
M = 256
FF = 2816
NFF = FF // P
GROUPS = (12, NFF - 12)
EPS = 1e-6
NEG = -1.0e30
TB = S // P
TILE = S
BLOCKS = 8
UNIT = BLOCKS * P
UNIT_S = 2 * P
SLOTS = 4
LEVELS = (64, 32, 16, 8, 4, 2, 1)
ZOFF = (0, 512, 1024, 896)
ZW = 1280
INV_FREQ = (np.float32(10000.0) ** (-np.arange(0, 64, 2, dtype=np.float32) / np.float32(64.0))).astype(np.float32)

F32 = mybir.dt.float32
F32R = mybir.dt.float32r
I32 = mybir.dt.int32
ALU = mybir.AluOpType
ACT = mybir.ActivationFunctionType
AX_X = mybir.AxisListType.X

_COLS = (
    ("g_mix_pre", 8), ("g_mem", 8), ("pool_scale", 4), ("g_mix_post", 8), ("g_ffn_pre", 8), ("g_ffn_post", 8),
    ("g_mix2_0", 8), ("g_mix2_1", 8), ("g_ffn2_0", 8), ("g_ffn2_1", 8), ("hgrn_lb", 8), ("g_hgrn_out", 1),
    ("g_qa", 2), ("g_kva", 2), ("g_q", 2), ("g_k", 2), ("conv_w0", 132), ("conv_b0", 44), ("conv_w1", 132),
    ("conv_b1", 44), ("w_mix", 512), ("ident", 128), ("ones", 128), ("neg_tri", 128), ("neg_ones", 128),
    ("sb_mask", 128), ("mla_mask", 128), ("levels", 1024), ("scan_keep", 512), ("pool_edge", 64),
    ("inv_freq", 1), ("swap", 128), ("eps", 1), ("one", 1), ("zero2", 2),
)
COL, NCOL = {}, 0
for _name, _n in _COLS:
    COL[_name] = NCOL
    NCOL += _n


class Count:

    START = 96

    def __init__(self, sem):
        self.sem, self.a, self.b = sem, self.START, 0

    def mark(self):
        return Mark(self, self.a, self.b)


class Mark:

    def __init__(self, count, a, b):
        self.count, self.a, self.b = count, a, b


class Absent:

    def nothing(self, *args, **kwargs):
        return None

    matmul = transpose = activation = tensor_tensor = tensor_scalar = tensor_copy = nothing
    scalar_tensor_tensor = tensor_tensor_scan = tensor_reduce = reciprocal = nothing


ABSENT = Absent()


class Schedule:
    def __init__(self, nc, ctx, mem, active, real):
        self.nc, self.m = nc, mem
        self.i, self.looping = 0, False
        self.active, self.real = active, real
        self.seen = {}
        self.pe = real if active == "pe" else ABSENT
        self.act = real if active == "act" else ABSENT
        self.dve = real if active == "dve" else ABSENT
        self.c = {n: Count(s) for n, s in mem.sems.items()}
        self.last = {}
        self.unit_a, self.unit_b = 0, 0

    def done(self, ins, name, by=1):
        c = self.c[name]
        if ins is not None:
            ins.then_inc(c.sem, by)
        c.a += by
        return Mark(c, c.a, c.b)

    def wait(self, eng, *marks):
        for mk in marks:
            if mk is not None:
                self.wait_value(eng, mk.count.sem, mk.a, mk.b)

    def wait_value(self, eng, sem, a, b):
        if eng is ABSENT:
            return
        key = id(sem)
        if b and self.looping:
            assert a > 0, "a wait's value stays positive"
            eng.wait_ge(sem, self.i * b + a)
        else:
            if self.seen.get(key, 0) >= a:
                return
            self.seen[key] = a
            eng.wait_ge(sem, a)

    def loop(self, n, body):
        before = {k: (c.a, c.b) for k, c in self.c.items()}
        unit, last = self.unit_a, dict(self.last)
        engines = self.pe, self.act, self.dve
        self.pe = self.act = self.dve = ABSENT
        body(0)
        self.pe, self.act, self.dve = engines
        step = {k: c.a - before[k][0] for k, c in self.c.items()}
        unit_step = self.unit_a - unit
        assert unit_step % SLOTS == 0
        names = {id(c): k for k, c in self.c.items()}
        carried = {k: mk for k, mk in self.last.items() if mk is not None and last.get(k) is not mk}
        for k in carried:
            if last.get(k) is not None:
                for e in engines:
                    self.wait(e, last[k])
        for k, c in self.c.items():
            c.a, c.b = before[k][0], step[k]
        self.unit_a, self.unit_b = unit, unit_step
        self.last = dict(last)
        for k, mk in carried.items():
            st = step[names[id(mk.count)]]
            self.last[k] = Mark(mk.count, mk.a - st, st)
        self.looping = True
        if self.real is None:
            body(0)
        else:
            with self.real.Fori(0, n) as i:
                self.i = i
                body(i)
        self.looping, self.i = False, 0
        for k, c in self.c.items():
            c.a, c.b = before[k][0] + n * step[k], 0
        self.unit_a, self.unit_b = unit + n * unit_step, 0
        for k, mk in self.last.items():
            if mk is not None and mk.b:
                self.last[k] = Mark(mk.count, mk.a + (n - 1) * mk.b, 0)


class Memory:

    def __init__(self, nc, ctx):
        sb = lambda n, w, d=F32: ctx.enter_context(nc.sbuf_tensor(n, [P, w], d))
        self.raw = sb("weights_raw", SLOTS * UNIT)
        self.wh = sb("weights_high", SLOTS * UNIT, F32R)
        self.wl = sb("weights_low", SLOTS * UNIT, F32R)
        self.h = sb("residual", KD * TILE)
        self.nh = sb("normed_high", KD * TILE, F32R)
        self.nl = sb("normed_low", KD * TILE, F32R)
        self.par = sb("parameters", NCOL)
        self.big = sb("scratch", 20 * TILE)
        self.bigr = sb("operands_high_low", 2 * 12 * TILE, F32R)
        self.ss = sb("sum_of_squares", TILE)
        self.sq = sb("squares", 2 * TILE)
        self.rstd = sb("rstd", TILE)
        self.small = sb("small", 64)
        self.g_bank = ctx.enter_context(nc.psum_tensor("ps_gemm", [P, 4 * 512], F32))
        self.a_bank = ctx.enter_context(nc.psum_tensor("ps_attend", [P, 4 * 512], F32))
        names = ("pe", "act", "dve", "hi", "use")
        self.sems = {n: ctx.enter_context(nc.semaphore(f"s_{n}")) for n in names}
        self.s_lo = ctx.enter_context(nc.semaphore("s_weights_low"))
        self.s_raw = [ctx.enter_context(nc.semaphore(f"s_raw{j}")) for j in range(SLOTS)]
        self.s_par = ctx.enter_context(nc.semaphore("s_parameters"))
        self.s_x = ctx.enter_context(nc.semaphore("s_x"))
        self.s_pos = ctx.enter_context(nc.semaphore("s_positions"))
        self.s_mem = ctx.enter_context(nc.semaphore("s_memory_input"))
        self.s_out = ctx.enter_context(nc.semaphore("s_outputs"))

    def col(self, name, k=0, n=1):
        c = COL[name]
        return self.par[:, bass.ds(k + c, n)] if not isinstance(k, int) else self.par[:, c + k:c + k + n]

    def gb(self, b, w=512, off=0):
        return self.g_bank[:, b * 512 + off:b * 512 + off + w]

    def ab(self, b, w=512, off=0):
        return self.a_bank[:, b * 512 + off:b * 512 + off + w]


HI_LEAD = 3


def hi_split(s, lead=HI_LEAD):
    m, act = s.m, s.act
    u, ub = s.unit_a + lead, s.unit_b
    if u >= s.n_units:
        return
    j = u % SLOTS
    w = UNIT_S if s.short(u) else UNIT
    s.wait_value(act, m.s_raw[j], 16 * (u // SLOTS + 1), 16 * (ub // SLOTS))
    s.wait_value(act, s.c["use"].sem, Count.START + u - SLOTS + 1, ub)
    ins = act.activation(m.wh[:, j * UNIT:j * UNIT + w], m.raw[:, j * UNIT:j * UNIT + w], ACT.Copy)
    s.done(ins, "hi")


def begin_unit(s):
    u, ub = s.unit_a, s.unit_b
    hi_split(s)
    s.wait_value(s.pe, s.c["hi"].sem, Count.START + u + 1, ub)
    s.wait_value(s.pe, s.m.s_lo, u + 1, ub)
    return (u % SLOTS) * UNIT


def end_unit(s, ins):
    s.unit_a += 1
    return s.done(ins, "use")


def products(s, out, base, pairs, start=True, stop=True):
    m, ins = s.m, None
    for n, (blk, xh, xl) in enumerate(pairs):
        c = base + blk * P
        for k, (w, x) in enumerate(((m.wh, xh), (m.wl, xh), (m.wh, xl))):
            ins = s.pe.matmul(out, w[:, c:c + P], x, start=start and n == 0 and k == 0,
                              stop=stop and n == len(pairs) - 1 and k == 2, skip_group_check=True)
    return ins


def full_tile(s, bank, xh, xl, width=TILE):
    base = begin_unit(s)
    s.wait(s.pe, s.last.get(("g", bank)))
    pairs = [(kb, xh[:, kb * width:(kb + 1) * width], xl[:, kb * width:(kb + 1) * width]) for kb in range(KD)]
    return end_unit(s, products(s, s.m.gb(bank, width), base, pairs))


def add_square(s, src, j, first, marks, width=TILE):
    m = s.m
    sl = m.sq[:, (j % 2) * TILE:(j % 2) * TILE + width]
    s.wait(s.act, *marks)
    if first:
        s.wait(s.act, s.last.get("ss"))
        sq = s.done(s.act.activation(m.ss[:, 0:width], src, ACT.Square), "act")
        s.last["ss_sum"] = sq
        return sq
    s.wait(s.act, s.last.get(("sq", j % 2)))
    sq = s.done(s.act.activation(sl, src, ACT.Square), "act")
    s.wait(s.dve, sq, s.last["ss_sum"])
    su = s.done(s.dve.tensor_tensor(m.ss[:, 0:width], m.ss[:, 0:width], sl, ALU.add), "dve")
    s.last[("sq", j % 2)] = su
    s.last["ss_sum"] = su
    return sq


def make_rstd(s, out, size, bank, ss=None, ss_mark=None, width=TILE):
    m = s.m
    own = ss is None
    ss = m.ss[:, 0:width] if own else ss
    ps = bank[0][:, 0:width]
    s.wait(s.pe, s.last["ss_sum"] if own else ss_mark, s.last.get(bank[1]))
    mm = s.done(s.pe.matmul(ps, m.col("ones", 0, P), ss, start=True, stop=True), "pe")
    if own:
        s.last["ss"] = mm
    s.wait(s.act, mm)
    ln = s.done(s.act.activation(out, ps, ACT.Ln, bias=m.col("eps"), scale=1.0 / size), "act")
    s.last[bank[1]] = ln
    s.wait(s.act, ln)
    return s.done(s.act.activation(out, out, ACT.Exp, scale=-0.5), "act"), mm


def split(s, high, low, src, mark, key=None):
    s.wait(s.act, mark, s.last.get(key) if key else None)
    hi = s.done(s.act.activation(high, src, ACT.Copy), "act")
    s.wait(s.dve, hi, mark)
    lo = s.done(s.dve.tensor_tensor(low, src, high.bitcast(F32), ALU.subtract), "dve")
    return hi, lo


def normed_input(s, gain, rstd_mark, src, high, low, temp, width=TILE):
    m, lo = s.m, None
    for j in range(KD):
        t = temp[:, (j % 2) * TILE:(j % 2) * TILE + width]
        x = src[:, j * width:(j + 1) * width]
        s.wait(s.dve, rstd_mark, s.last.get(("sq", j % 2)), s.last.get("h"))
        n = s.done(s.dve.scalar_tensor_tensor(out=t, in0=x, scalar=m.col(gain, j), in1=m.rstd[:, 0:width],
                                              op0=ALU.mult, op1=ALU.mult), "dve")
        sl = slice(j * width, (j + 1) * width)
        _, lo = split(s, high[:, sl], low[:, sl], t, n, "n_read")
        s.last[("sq", j % 2)] = lo
    s.wait(s.pe, lo)
    return lo


def A(s, k):
    return (s.m.ab(k), ("a", k))


def G(s, k):
    return (s.m.gb(k), ("g", k))


def attend_banks_free(s):
    s.wait(s.pe, *(s.last.get(("a", k)) for k in range(4)))


def project_out(s, xh, xl, into):
    for j in range(KD):
        pe = full_tile(s, j % 4, xh, xl)
        into(j, s.m.gb(j % 4), pe, ("g", j % 4))
    s.last["n_read"] = pe


def residual_add(s, j, ps, pe, key):
    m = s.m
    h = m.h[:, j * TILE:(j + 1) * TILE]
    s.wait(s.dve, pe, s.last.get("h"))
    a = s.done(s.dve.tensor_tensor(h, h, ps, ALU.add), "dve")
    s.last[key] = a
    s.last["h_new"] = a
    add_square(s, h, j, j == 0, (a,))


def keep_branch(s, j, ps, pe, key, acc=None):
    m = s.m
    f = m.big[:, j * TILE:(j + 1) * TILE]
    if acc is None:
        s.wait(s.act, pe, s.last.get("f"))
        a = s.done(s.act.activation(f, ps, ACT.Copy), "act")
    else:
        s.wait(s.dve, pe, acc)
        a = s.done(s.dve.tensor_tensor(f, f, ps, ALU.add), "dve")
    s.last[key] = a
    add_square(s, f, j, j == 0, (a,))
    return a


def post_norm_add(s, gain):
    m = s.m
    s.wait(s.act, s.last.get("rstd_read"))
    r, _ = make_rstd(s, m.rstd[:, :], D, A(s, 3))
    for j in range(KD):
        sl = slice(j * TILE, (j + 1) * TILE)
        f, h = m.big[:, sl], m.h[:, sl]
        s.wait(s.dve, r)
        a = s.done(s.dve.scalar_tensor_tensor(out=f, in0=f, scalar=m.col(gain, j), in1=m.rstd[:, :],
                                              op0=ALU.mult, op1=ALU.mult), "dve")
        s.wait(s.dve, a)
        a = s.done(s.dve.tensor_tensor(h, h, f, ALU.add), "dve")
        s.last["f"] = a
        s.last["rstd_read"] = a
        add_square(s, h, j, j == 0, (a,))
    s.last["h_new"] = a


def pre_norm(s, gain):
    m = s.m
    s.wait(s.act, s.last.get("rstd_read"))
    r, _ = make_rstd(s, m.rstd[:, :], D, A(s, 3))
    lo = normed_input(s, gain, r, m.h, m.nh, m.nl, m.sq)
    s.last["rstd_read"] = lo


def feed_forward(s, conv, read_out):
    m = s.m
    y = [m.big[:, (8 + k) * TILE:(9 + k) * TILE] for k in range(4)]
    tile0 = 0
    for group, n in enumerate(GROUPS):
        def up_pair(k, idx):
            for half in range(2):
                b = 2 * k + half
                pe = full_tile(s, b, m.nh, m.nl)
                ps, out = m.gb(b), y[b]
                if conv is None:
                    if half == 0:
                        s.wait(s.act, pe, s.last.get(("y", b)))
                        e = s.done(s.act.activation(out, ps, ACT.Silu), "act")
                        gate, s.last[("g", b)] = e, e
                    else:
                        t = y[2 * k]
                        s.wait(s.dve, pe, gate)
                        prod = s.done(s.dve.tensor_tensor(t, t, ps, ALU.mult), "dve")
                        s.last[("g", b)] = prod
                else:
                    c = 22 * half + tile0
                    w = lambda tap: m.col(f"conv_w{conv}", idx + (44 * tap + c))
                    s.wait(s.act, pe, s.last.get(("y", b)))
                    e = s.done(s.act.activation(out, ps, ACT.Identity, bias=m.col(f"conv_b{conv}", idx + c),
                                                scale=w(2)), "act")
                    s.wait(s.dve, e)
                    e = s.done(s.dve.scalar_tensor_tensor(out=out[:, 1:S], in0=ps[:, 0:S - 1], scalar=w(1),
                                                          in1=out[:, 1:S], op0=ALU.mult, op1=ALU.add), "dve")
                    s.wait(s.dve, e)
                    e = s.done(s.dve.scalar_tensor_tensor(out=out[:, 2:S], in0=ps[:, 0:S - 2], scalar=w(0),
                                                          in1=out[:, 2:S], op0=ALU.mult, op1=ALU.add), "dve")
                    s.last[("g", b)] = e
                    if half == 0:
                        s.wait(s.act, e)
                        gate = s.done(s.act.activation(out, out, ACT.Silu), "act")
                    else:
                        s.wait(s.dve, gate, e)
                        prod = s.done(s.dve.tensor_tensor(y[2 * k], y[2 * k], out, ALU.mult), "dve")
                        s.last[("y", b)] = prod
            cols = bass.ds(idx * TILE, TILE)
            low = bass.ds(idx * TILE + 12 * TILE, TILE)
            _, lo = split(s, m.bigr[:, cols], m.bigr[:, low], y[2 * k], prod, "ff_read")
            s.last[("y", 2 * k)] = lo
            s.last["ff"] = lo

        def up_body(i):
            for k in range(2):
                up_pair(k, i * 2 + k)
        s.loop(n // 2, up_body)
        s.wait(s.pe, s.last["ff"])
        for b in range(KD):
            ps, key = (G(s, b) if b < 4 else A(s, b - 4))
            s.wait(s.pe, s.last.get(key))
            s.pe.matmul(ps[:, 0:2], m.col("ident", 0, P), m.col("zero2", 0, 2), start=True, stop=False,
                        skip_group_check=True)

        def down_unit(k, idx):
            base = begin_unit(s)
            xh = m.bigr[:, bass.ds(idx * TILE, TILE)]
            xl = m.bigr[:, bass.ds(idx * TILE + 12 * TILE, TILE)]
            for b in range(KD):
                ps = m.gb(b) if b < 4 else m.ab(b - 4)
                ins = products(s, ps, base, [(b, xh, xl)], start=False, stop=False)
            return end_unit(s, ins)

        def down_body(i):
            for k in range(4):
                s.last["ff_read"] = down_unit(k, i * 4 + k)
        rounds = n // 4 - (s.unit_a + n - n % 4 + HI_LEAD > s.n_units)
        s.loop(rounds, down_body)
        for k in range(4 * rounds, n):
            s.last["ff_read"] = down_unit(k, k)
        for j in range(KD):
            ps, key = (G(s, j) if j < 4 else A(s, j - 4))
            read_out(group, j, ps, s.last["ff_read"], key)
        tile0 += n
    s.last["n_read"] = s.last["ff_read"]


def to_tokens(s, dst, src, mark, bank, key):
    m, nb = s.m, src.shape[1] // P
    s.wait(s.pe, mark, s.last.get(bank[1]))
    for b in range(nb):
        ins = s.pe.transpose(bank[0][:, b * P:(b + 1) * P], src[:, b * P:(b + 1) * P], m.col("ident", 0, P))
    t = s.done(ins, "pe")
    s.wait(s.act, t, s.last.get(key))
    e = s.done(s.act.activation(dst, bank[0][:, 0:nb * P], ACT.Copy), "act")
    s.last[bank[1]] = e
    return e


def copy_out(s, dst, bank, pe, key=None, scale=1.0):
    s.wait(s.act, pe, s.last.get(key) if key else None)
    e = s.done(s.act.activation(dst, bank[0][:, 0:dst.shape[1]], ACT.Copy, scale=scale), "act")
    s.last[bank[1]] = e
    return e


def memory_keys_values(s):
    m = s.m
    mem = m.big[:, 4 * TILE:8 * TILE]
    for e in (s.act, s.dve, s.pe):
        s.wait_value(e, m.s_par, 16, 0)
    s.wait_value(s.act, m.s_mem, 16, 0)
    for j in range(KD):
        add_square(s, mem[:, j * M:(j + 1) * M], j, j == 0, (), M)
    r, _ = make_rstd(s, m.rstd[:, 0:M], D, A(s, 3), width=M)
    s.wait_value(s.dve, m.s_mem, 16, 0)
    high, low = m.bigr[:, 0:KD * M], m.bigr[:, KD * M:2 * KD * M]
    lo = normed_input(s, "g_mem", r, mem, high, low, m.sq, M)
    s.last["rstd_read"] = lo
    keys, vt, vals = m.big[:, 0:2 * M], m.big[:, 2 * M:4 * M], m.big[:, 4 * M:6 * M]
    for j in range(4):
        pe = full_tile(s, j, high, low, M)
        dst = (keys, vt)[j // 2][:, (j % 2) * M:(j % 2 + 1) * M]
        e = copy_out(s, dst, G(s, j), pe)
        if j < 2:
            s.last["mem_keys"] = e
        else:
            s.last["mem_vals"] = to_tokens(s, vals[:, (j - 2) * M:(j - 1) * M], dst, e, A(s, 2), None)
    s.last["mem_read"] = pe


def pool_mixer(s):
    m = s.m
    a, b = m.big[:, 9 * TILE:10 * TILE], m.big[:, 10 * TILE:11 * TILE]
    p = m.big[:, 8 * TILE:9 * TILE]
    for g in range(4):
        pe = full_tile(s, g, m.nh, m.nl)
        e = copy_out(s, p, G(s, g), pe, "pool_p")
        src, dst, last = p, a, e
        for k in range(g + 1):
            w = 1 << k
            s.wait(s.dve, last, s.last.get("pool_ab"), s.last.get("pool_out"))
            s.done(s.dve.tensor_copy(dst[:, 0:w], src[:, 0:w]), "dve")
            last = s.done(s.dve.tensor_tensor(dst[:, w:S], src[:, w:S], src[:, 0:S - w], ALU.add), "dve")
            src, dst = dst, (b if dst is a else a)
        s.wait(s.dve, last)
        edge = s.done(s.dve.tensor_tensor(src[:, 0:16], src[:, 0:16], m.col("pool_edge", 16 * g, 16), ALU.mult), "dve")
        s.wait(s.dve, edge)
        mix = s.done(s.dve.scalar_tensor_tensor(out=src, in0=src, scalar=1.0 / (2 << g), in1=p,
                                                op0=ALU.mult, op1=ALU.subtract), "dve")
        s.last["pool_p"] = mix
        s.wait(s.pe, mix, s.last.get(("a", 3)))
        mm = s.done(s.pe.matmul(m.ab(3), m.col("w_mix", g * P, P), src, start=True, stop=True), "pe")
        s.last["pool_ab"] = mm
        s.wait(s.act, mm)
        y = s.done(s.act.activation(dst, m.ab(3), ACT.Identity, scale=m.col("pool_scale", g)), "act")
        s.last[("a", 3)] = y
        o = (2 * KD * M) + g * TILE
        _, lo = split(s, m.bigr[:, o:o + TILE], m.bigr[:, o + 4 * TILE:o + 5 * TILE], dst, y)
        s.last["pool_out"] = lo


def memory_attention(s):
    m = s.m
    keys, vals = m.big[:, 0:2 * M], m.big[:, 4 * M:6 * M]
    xq = m.big[:, 4 * TILE:6 * TILE]
    prob = m.big[:, 6 * TILE:8 * TILE]
    pt = m.big[:, 8 * TILE:16 * TILE]
    s.wait(s.act, s.last["mem_vals"])
    for j in range(2):
        pe = full_tile(s, j, m.nh, m.nl)
        e = copy_out(s, xq[:, j * TILE:(j + 1) * TILE], G(s, j), pe, "xq_free")
    s.wait(s.pe, e, s.last["mem_keys"], s.last["pool_out"])
    mx, nb, sm = m.small[:, 0:4], m.small[:, 4:8], m.small[:, 8:12]
    for tb in range(TB):
        s.wait(s.pe, s.last.get(("a", 0)), s.last.get(("a", 1)))
        for h in range(4):
            r, tile = 64 * (h % 2), h // 2
            out = m.ab(h % 2, M, (h // 2) * M)
            ins = s.pe.matmul(out, xq[r:r + 64, tile * TILE + tb * P:tile * TILE + (tb + 1) * P],
                              keys[r:r + 64, tile * M:(tile + 1) * M], start=h < 2, stop=h >= 2, skip_group_check=True)
        mm = s.done(ins, "pe")
        s.wait(s.dve, mm, s.last.get("x_small"))
        sc = m.a_bank[:, 0:4 * M].rearrange("p (h m) -> p h m", h=4)
        d = s.done(s.dve.tensor_reduce(mx, sc, AX_X, ALU.max), "dve")
        s.wait(s.dve, d)
        d = s.done(s.dve.tensor_scalar(nb, mx, -0.125, None, ALU.mult), "dve")
        s.wait(s.act, d, s.last.get("prob"))
        for h in range(4):
            e = s.done(s.act.activation(prob[:, h * M:(h + 1) * M], m.a_bank[:, h * M:(h + 1) * M], ACT.Exp,
                                        bias=nb[:, h:h + 1], scale=0.125, accum_out=sm[:, h:h + 1]), "act")
        s.last[("a", 0)] = s.last[("a", 1)] = e
        s.wait(s.dve, e)
        d = s.done(s.dve.reciprocal(sm, sm), "dve")
        s.wait(s.dve, d)
        for h in range(4):
            d = s.done(s.dve.tensor_scalar(prob[:, h * M:(h + 1) * M], prob[:, h * M:(h + 1) * M],
                                           sm[:, h:h + 1], None, ALU.mult), "dve")
        s.last["x_small"] = d
        s.wait(s.pe, d, s.last.get(("a", 2)), s.last.get(("a", 3)))
        for k in range(8):
            ins = s.pe.transpose(m.ab(2 + k // 4, P, (k % 4) * P), prob[:, k * P:(k + 1) * P], m.col("ident", 0, P))
        t = s.done(ins, "pe")
        s.last["prob"] = t
        s.wait(s.act, t)
        dst = pt.rearrange("p (k t) -> p k t", k=8)[:, :, tb * P:(tb + 1) * P]
        e = s.done(s.act.activation(dst, m.a_bank[:, 1024:2048].rearrange("p (k t) -> p k t", k=8), ACT.Copy), "act")
        s.last[("a", 2)] = s.last[("a", 3)] = e
    s.wait(s.pe, e)
    for j in range(2):
        s.wait(s.pe, s.last.get(("a", j)))
        for h in (2 * j, 2 * j + 1):
            k = (h % 2) * 2 + h // 2
            r = 64 * (h % 2)
            for mb in range(2):
                ins = s.pe.matmul(m.a_bank[r:r + 64, j * 512:(j + 1) * 512],
                                  vals[:, j * M + mb * P + r:j * M + mb * P + r + 64],
                                  pt[:, (2 * k + mb) * TILE:(2 * k + mb + 1) * TILE], start=mb == 0, stop=mb == 1,
                                  skip_group_check=True)
        mm = s.done(ins, "pe")
        s.wait(s.act, s.last["mem_read"])
        _, lo = split(s, m.bigr[:, j * TILE:(j + 1) * TILE], m.bigr[:, (2 + j) * TILE:(3 + j) * TILE], m.ab(j), mm)
        s.last[("a", j)] = lo
    s.last["x_out"] = lo


def cross_branch_out(s):
    m = s.m
    y = m.big[:, 0:KD * TILE]
    s.wait(s.pe, s.last["x_out"])
    for u in range(2):
        base = begin_unit(s)
        for k in range(4):
            s.wait(s.pe, s.last.get(("g", k)))
            pairs = [(2 * k + kb, m.bigr[:, kb * TILE:(kb + 1) * TILE], m.bigr[:, (2 + kb) * TILE:(3 + kb) * TILE])
                     for kb in range(2)]
            ins = products(s, m.gb(k), base, pairs)
            if k < 3:
                pe = s.done(ins, "pe")
            else:
                pe = end_unit(s, ins)
            j = 4 * u + k
            s.last["merged"] = copy_out(s, y[:, j * TILE:(j + 1) * TILE], G(s, k), pe)
    s.last["x_read"] = pe


def stick_breaking(s):
    m = s.m
    c0 = KD * TILE
    q, k, vt = (m.big[:, c0 + n * TILE:c0 + (n + 1) * TILE] for n in range(3))
    vtok = m.big[:, c0 + 3 * TILE:c0 + 4 * TILE]
    c1 = c0 + 4 * TILE
    lg = [m.big[:, c1 + n * ZW:c1 + (n + 1) * ZW] for n in range(2)]
    gate = [m.sq[:, 0:TILE], m.sq[:, TILE:2 * TILE]]
    at = m.ss[:, :]
    zb = m.a_bank[:, 0:ZW]
    o_high, o_low = 2 * KD * M + 8 * TILE, 2 * KD * M + 12 * TILE

    def body(i):
        for n, (dst, scale) in enumerate(((q, 0.125), (k, 1.0), (vt, 1.0))):
            pe = full_tile(s, n, m.nh, m.nl)
            e = copy_out(s, dst, G(s, n), pe, ("sb", n), scale)
        e_v = to_tokens(s, vtok, vt, e, A(s, 3), "vtok")
        s.last[("sb", 2)] = e_v

        def scores(hh):
            r = 64 * hh
            s.wait(s.pe, e, s.last.get(("a", 0)))
            for kb in (0, 1, 3, 2):
                w = S - kb * P
                s.pe.matmul(zb[:, ZOFF[kb]:ZOFF[kb] + w], k[r:r + 64, kb * P:(kb + 1) * P], q[r:r + 64, kb * P:S],
                            start=kb != 3, stop=False, skip_group_check=True)
            for kb in range(TB):
                ins = s.pe.matmul(zb[:, ZOFF[kb]:ZOFF[kb] + P], m.col("ident", 0, P), m.col("sb_mask", 0, P),
                                  start=False, stop=False, skip_group_check=True)
            return s.done(ins, "pe")

        def softplus(hh, mm):
            x = lg[hh]
            s.wait(s.act, mm, s.last.get(("lg", hh)))
            e0 = s.done(s.act.activation(x, zb, ACT.Abs), "act")
            s.wait(s.act, e0)
            e1 = s.done(s.act.activation(x, x, ACT.Exp, scale=-1.0), "act")
            s.wait(s.act, e1)
            e2 = s.done(s.act.activation(x, x, ACT.Ln, bias=m.col("one")), "act")
            s.wait(s.dve, e2)
            return s.done(s.dve.scalar_tensor_tensor(out=x, in0=zb, scalar=0.0, in1=x, op0=ALU.max, op1=ALU.add), "dve")

        def suffix(hh, d):
            x = lg[hh]
            s.wait(s.pe, d)
            for kb in range(TB):
                for j in range(kb, TB):
                    lhs = m.col("neg_tri" if j == kb else "neg_ones", 0, P)
                    o = ZOFF[kb] + (j - kb) * P
                    ins = s.pe.matmul(zb[:, o:o + S - j * P], lhs, x[:, ZOFF[j]:ZOFF[j] + S - j * P], start=False,
                                      stop=False, skip_group_check=True)
            mm = s.done(ins, "pe")
            s.wait(s.act, mm)
            e3 = s.done(s.act.activation(x, zb, ACT.Exp), "act")
            s.last[("a", 0)] = e3
            return e3

        def values(hh, e3):
            r = 64 * hh
            x = lg[hh]
            s.wait(s.pe, e3, e_v, s.last.get(("a", 3)))
            for kb in range(TB):
                ins = s.pe.matmul(m.a_bank[r:r + 64, 3 * 512 + kb * P:4 * 512], vtok[:, kb * P + r:kb * P + r + 64],
                                  x[:, ZOFF[kb]:ZOFF[kb] + S - kb * P], start=kb == 0, stop=kb == 3,
                                  skip_group_check=True)
            mm = s.done(ins, "pe")
            s.last[("lg", hh)] = mm
            return mm

        def pooled(half, ctx, base):
            g0, d, cols = ctx
            s.wait(s.pe, s.last.get(("g", 2 + half)))
            o = 2 * KD * M
            pairs = [(4 * half + kb, m.bigr[:, o + kb * TILE:o + (kb + 1) * TILE],
                      m.bigr[:, o + (4 + kb) * TILE:o + (5 + kb) * TILE]) for kb in range(4)]
            ins = products(s, m.gb(2 + half), base, pairs)
            pe = end_unit(s, ins) if half else s.done(ins, "pe")
            s.wait(s.dve, pe, g0)
            t = s.done(s.dve.tensor_tensor(gate_keep[half], gate_keep[half], m.gb(2 + half), ALU.mult), "dve")
            s.last[("g", 2 + half)] = t
            s.wait(s.dve, t, d)
            y = m.big[:, cols]
            t = s.done(s.dve.tensor_tensor(y, y, gate_keep[half], ALU.add), "dve")
            s.last[keep_key[half]] = t
            return t

        gate_keep, keep_key = [m.rstd[:, :], at], ["rstd_read", "ss"]
        ctxs = []

        def gates_of(half):
            cols = bass.ds((i * 2 + half) * TILE, TILE)
            pe = full_tile(s, 0, m.nh, m.nl)
            s.wait(s.act, pe, s.last.get(keep_key[half]))
            g0 = s.done(s.act.activation(gate_keep[half], m.gb(0), ACT.Sigmoid), "act")
            s.last[("g", 0)] = g0
            pe = full_tile(s, 1, m.nh, m.nl)
            s.wait(s.act, pe, s.last.get(("sq", half)))
            g2 = s.done(s.act.activation(gate[half], m.gb(1), ACT.Sigmoid), "act")
            s.last[("g", 1)] = g2
            y = m.big[:, cols]
            s.wait(s.dve, g2)
            d = s.done(s.dve.tensor_tensor(y, y, gate[half], ALU.mult), "dve")
            s.last[("sq", half)] = d
            ctxs.append((g0, d, cols))

        d0 = softplus(0, scores(0))
        gates_of(0)
        x0 = suffix(0, d0)
        d1 = softplus(1, scores(1))
        values(0, x0)
        gates_of(1)
        x1 = suffix(1, d1)
        base = begin_unit(s)
        pooled(0, ctxs[0], base)
        s.last["merged"] = pooled(1, ctxs[1], base)
        mm = values(1, x1)
        s.last[("sb", 0)] = s.last[("sb", 1)] = s.last["vtok"] = mm
        _, lo = split(s, m.bigr[:, bass.ds(i * TILE + o_high, TILE)], m.bigr[:, bass.ds(i * TILE + o_low, TILE)],
                      m.ab(3), mm)
        s.last[("a", 3)] = lo
        s.last["sb_out"] = lo

    s.wait(s.dve, s.last["merged"])
    attend_banks_free(s)
    s.loop(4, body)
    s.last[("a", 1)] = s.last[("a", 2)] = s.last[("a", 0)]


def merge_branches(s):
    m = s.m
    o_high, o_low = 2 * KD * M + 8 * TILE, 2 * KD * M + 12 * TILE
    for j in range(0, KD, 2):
        gates = []
        for n in range(2):
            pe = full_tile(s, n, m.nh, m.nl)
            gt = m.sq[:, n * TILE:(n + 1) * TILE]
            s.wait(s.act, pe, s.last.get(("sq", n)))
            e = s.done(s.act.activation(gt, m.gb(n), ACT.Sigmoid), "act")
            s.last[("g", n)] = e
            gates.append(e)
        base = begin_unit(s)
        s.wait(s.pe, s.last["sb_out"])
        for n in range(2):
            gt = m.sq[:, n * TILE:(n + 1) * TILE]
            s.wait(s.pe, s.last.get(("g", 2 + n)))
            pairs = [(4 * n + kb, m.bigr[:, o_high + kb * TILE:o_high + (kb + 1) * TILE],
                      m.bigr[:, o_low + kb * TILE:o_low + (kb + 1) * TILE]) for kb in range(4)]
            ins = products(s, m.gb(2 + n), base, pairs)
            pe = end_unit(s, ins) if n else s.done(ins, "pe")
            y = m.big[:, (j + n) * TILE:(j + n + 1) * TILE]
            s.wait(s.dve, pe, gates[n], s.last["merged"])
            t = s.done(s.dve.tensor_tensor(gt, gt, m.gb(2 + n), ALU.mult), "dve")
            s.last[("g", 2 + n)] = t
            s.wait(s.dve, t)
            t = s.done(s.dve.tensor_tensor(y, y, gt, ALU.add), "dve")
            s.last[("sq", n)] = t
            s.last["merged"] = t
    s.last["n_read"] = pe
    for j in range(KD):
        sl = slice(j * TILE, (j + 1) * TILE)
        _, lo = split(s, m.nh[:, sl], m.nl[:, sl], m.big[:, sl], s.last["merged"], "n_read")
    s.wait(s.pe, lo)
    s.last["f"] = lo


def first_block(s):
    m = s.m
    memory_keys_values(s)
    s.wait_value(s.act, m.s_x, 16, 0)
    s.wait_value(s.dve, m.s_x, 16, 0)
    for j in range(KD):
        add_square(s, m.h[:, j * TILE:(j + 1) * TILE], j, j == 0, ())
    pre_norm(s, "g_mix_pre")
    pool_mixer(s)
    memory_attention(s)
    cross_branch_out(s)
    stick_breaking(s)
    merge_branches(s)
    project_out(s, m.nh, m.nl, lambda j, ps, pe, key: keep_branch(s, j, ps, pe, key))
    s.last["ff_read"] = s.last["n_read"]
    post_norm_add(s, "g_mix_post")
    pre_norm(s, "g_ffn_pre")

    def read_out(group, j, ps, pe, key):
        if group == 0:
            f = m.big[:, j * TILE:(j + 1) * TILE]
            s.wait(s.act, pe, s.last.get("f"))
            e = s.done(s.act.activation(f, ps, ACT.Copy), "act")
            s.last[key] = e
            s.last["f_acc"] = e
        else:
            keep_branch(s, j, ps, pe, key, acc=s.last["f_acc"])
    feed_forward(s, None, read_out)
    post_norm_add(s, "g_ffn_post")


def lower_bounds(s):
    m = s.m
    lb, e, oml = m.small[:, 16:24], m.small[:, 24:32], m.small[:, 32:40]
    raw = m.col("hgrn_lb", 0, 8)
    d = s.done(s.dve.tensor_tensor(e, raw, raw, ALU.subtract), "dve")
    s.wait(s.act, d)
    x = s.done(s.act.activation(e, e, ACT.Exp), "act")
    s.wait(s.dve, x)
    d = s.done(s.dve.reciprocal(lb, e), "dve")
    s.wait(s.dve, d)
    d = s.done(s.dve.tensor_tensor(e, e, lb, ALU.mult), "dve")
    s.wait(s.dve, d)
    d = s.done(s.dve.tensor_tensor(lb, e, e, ALU.subtract), "dve")
    s.wait(s.dve, d)
    s.last["lb"] = s.done(s.dve.tensor_scalar(oml, lb, -1.0, 1.0, ALU.mult, ALU.add), "dve")


def recurrence(s):
    m = s.m
    t = lambda k, n=1: m.big[:, k * TILE:(k + n) * TILE]
    key, qs, cum, sg, vt, vtok, diag, eg, kb_, tmp, o = (t(k) for k in range(11))
    xs = [t(11), t(12)]
    cross = m.big[:, 13 * TILE:13 * TILE + 768]
    qf, k0, q3 = t(15), m.big[:, 16 * TILE:16 * TILE + P], m.big[:, 16 * TILE + P:16 * TILE + 2 * P]
    blocks = lambda ap: ap.rearrange("p (c t) -> p c t", c=TB)
    s.wait(s.dve, s.last["lb"])

    def project(i):
        pe = full_tile(s, 0, m.nh, m.nl)
        s.wait(s.act, pe, s.last.get("tmp"))
        e = s.done(s.act.activation(tmp, m.gb(0), ACT.Sigmoid), "act")
        s.last[("g", 0)] = e
        s.wait(s.dve, e)
        d = s.done(s.dve.tensor_scalar(tmp, tmp, m.small[:, bass.ds(i + 32, 1)], m.small[:, bass.ds(i + 16, 1)],
                                       ALU.mult, ALU.add), "dve")
        s.wait(s.dve, d, s.last.get("levels_read"))
        s.done(s.dve.tensor_scalar(key, tmp, -1.0, 1.0, ALU.mult, ALU.add), "dve")
        d = s.done(s.dve.tensor_scalar(tmp, tmp, 2.0 ** -63, None, ALU.max), "dve")
        pe = full_tile(s, 1, m.nh, m.nl)
        s.wait(s.act, pe, s.last.get("levels_read"))
        e_q = s.done(s.act.activation(qs, m.gb(1), ACT.Silu), "act")
        s.last[("g", 1)] = e_q
        s.wait(s.act, d)
        e = s.done(s.act.activation(tmp, tmp, ACT.Ln), "act")
        s.wait(s.dve, e)
        d = s.done(s.dve.tensor_tensor_scan(cum, m.col("scan_keep", 0, S), tmp, 0.0, ALU.mult, ALU.add), "dve")
        s.last["tmp"] = d
        return e_q, d

    def values_and_gate(i):
        pe = full_tile(s, 2, m.nh, m.nl)
        e = copy_out(s, vt, G(s, 2), pe, "vt")
        pe = full_tile(s, 3, m.nh, m.nl)
        s.wait(s.act, pe, s.last.get("sg"))
        s.last["n_read"] = pe
        e_g = s.done(s.act.activation(sg, m.gb(3), ACT.Silu), "act")
        s.last[("g", 3)] = e_g
        s.last["sg_ready"] = e_g
        return e

    def pair_factors(w, buf, n2, e_q, c):
        v = lambda ap: ap.rearrange("p (n a w) -> p n a w", a=2, w=w)
        g, x = v(cum), v(buf)
        mid = g[:, :, 0, w - 1:w].broadcast_to([P, S // (2 * w), w])
        s.wait(s.dve, c, s.last.get(("xs", n2)))
        s.done(s.dve.tensor_tensor(x[:, :, 0, :], mid, g[:, :, 0, :], ALU.subtract), "dve")
        d = s.done(s.dve.tensor_tensor(x[:, :, 1, :], g[:, :, 1, :], mid, ALU.subtract), "dve")
        s.wait(s.act, d)
        e = s.done(s.act.activation(buf, buf, ACT.Exp), "act")
        s.wait(s.dve, e, e_q)
        s.done(s.dve.tensor_tensor(x[:, :, 0, :], x[:, :, 0, :], v(key)[:, :, 0, :], ALU.mult), "dve")
        return s.done(s.dve.tensor_tensor(x[:, :, 1, :], x[:, :, 1, :], v(qs)[:, :, 1, :], ALU.mult), "dve")

    def masked_level(n, left, right, mark, bank):
        s.wait(s.pe, mark, s.last.get(("a", bank)))
        for c in range(TB):
            ins = s.pe.matmul(m.ab(bank, P, c * P), left[:, c * P:(c + 1) * P], right[:, c * P:(c + 1) * P],
                              start=c == 0, stop=c == TB - 1, skip_group_check=True)
        mm = s.done(ins, "pe")
        mask = m.col("levels", n * P, P).unsqueeze(1).broadcast_to([P, TB, P])
        s.wait(s.dve, mm)
        if n == 0:
            s.wait(s.dve, s.last.get("diag"))
            d = s.done(s.dve.tensor_tensor(blocks(diag), blocks(m.ab(bank)), mask, ALU.mult), "dve")
            s.last[("a", bank)] = d
        else:
            s.wait(s.dve, s.last.get(("sq", n % 2)))
            d = s.done(s.dve.tensor_tensor(blocks(mt[n % 2]), blocks(m.ab(bank)), mask, ALU.mult), "dve")
            s.last[("a", bank)] = d
            s.wait(s.dve, d, s.last["diag_sum"])
            d = s.done(s.dve.tensor_tensor(diag, diag, mt[n % 2], ALU.add), "dve")
            s.last[("sq", n % 2)] = d
        s.last["diag_sum"] = d
        return mm

    mt = [m.sq[:, 0:TILE], m.sq[:, TILE:2 * TILE]]

    def levels(e_q, c):
        s.wait(s.act, c, s.last.get("eg"))
        e = s.done(s.act.activation(eg, cum, ACT.Exp), "act")
        s.wait(s.dve, c, s.last.get("cross_read"))
        last = blocks(cum)[:, :, P - 1:P].broadcast_to([P, TB, P])
        d = s.done(s.dve.tensor_tensor(blocks(kb_), last, blocks(cum), ALU.subtract), "dve")
        s.wait(s.act, d)
        e2 = s.done(s.act.activation(kb_, kb_, ACT.Exp), "act")
        s.wait(s.dve, e, e_q)
        d = s.done(s.dve.tensor_tensor(qf, qs, eg, ALU.mult), "dve")
        s.wait(s.dve, e2)
        d2 = s.done(s.dve.tensor_tensor(kb_, kb_, key, ALU.mult), "dve")
        s.wait(s.dve, d, d2)
        s.done(s.dve.tensor_scalar(k0, kb_[:, 0:P], eg[:, 2 * P - 1:2 * P], None, ALU.mult), "dve")
        d = s.done(s.dve.tensor_scalar(q3, qf[:, 3 * P:4 * P], eg[:, 3 * P - 1:3 * P], None, ALU.mult), "dve")
        s.last["eg"] = d
        masked_level(0, key, qs, d, 0)
        for n, w in enumerate(LEVELS):
            buf = xs[n % 2]
            f = pair_factors(w, buf, n % 2, e_q, c)
            mm = masked_level(n + 1, buf, buf, f, 0 if n % 2 else 3)
            s.last[("xs", n % 2)] = mm
        s.last["levels_read"] = s.last["diag_sum"]
        s.wait(s.pe, s.last.get(("a", 1)))
        for kk, qq, out, first in ((kb_[:, 0:P], qf[:, P:2 * P], 0, 1), (k0, qf[:, 2 * P:3 * P], 128, 0),
                                   (k0, q3, 256, 0), (kb_[:, P:2 * P], qf[:, 2 * P:3 * P], 384, 0),
                                   (kb_[:, P:2 * P], q3, 512, 1),
                                   (kb_[:, 2 * P:3 * P], qf[:, 3 * P:4 * P], 640, 0)):
            ins = s.pe.matmul(m.ab(1, P, out), kk, qq, start=bool(first), stop=False, skip_group_check=True)
        mm = s.done(ins, "pe")
        s.last["cross_read"] = mm
        s.wait(s.act, mm, s.last.get("cross"))
        e = s.done(s.act.activation(cross, m.ab(1, 768), ACT.Copy), "act")
        s.last[("a", 1)] = e
        s.last["cross_ready"] = e

    def attend(i, tok):
        s.wait(s.pe, tok, s.last["diag_sum"], s.last["cross_ready"], s.last.get(("a", 3)))
        for c in range(TB):
            s.pe.matmul(m.ab(3, P, c * P), vtok[:, c * P:(c + 1) * P], diag[:, c * P:(c + 1) * P], start=c == 0,
                        stop=False, skip_group_check=True)
        for c, a, b in ((0, 0, 384), (1, 384, 640), (2, 640, 768)):
            ins = s.pe.matmul(m.ab(3, b - a, (c + 1) * P), vtok[:, c * P:(c + 1) * P], cross[:, a:b], start=False,
                              stop=c == 2, skip_group_check=True)
        mm = s.done(ins, "pe")
        s.last["vtok"] = s.last["diag"] = s.last["cross"] = mm
        s.wait(s.act, mm, s.last.get("ss"))
        q = s.done(s.act.activation(m.ss[:, :], m.ab(3), ACT.Square), "act")
        s.wait(s.act, s.last.get("o"))
        oc = s.done(s.act.activation(o, m.ab(3), ACT.Copy), "act")
        s.last[("a", 3)] = oc
        s.wait(s.act, s.last.get("rstd_read"))
        r, mm2 = make_rstd(s, m.rstd[:, :], P, A(s, 3), m.ss[:, :], q)
        s.last["ss"] = mm2
        s.wait(s.dve, r, oc)
        d = s.done(s.dve.scalar_tensor_tensor(out=o, in0=o, scalar=m.col("g_hgrn_out"), in1=m.rstd[:, :],
                                              op0=ALU.mult, op1=ALU.mult), "dve")
        s.last["rstd_read"] = d
        s.wait(s.dve, d, s.last["sg_ready"])
        d = s.done(s.dve.tensor_tensor(o, o, sg, ALU.mult), "dve")
        s.last["sg"] = d
        _, lo = split(s, m.bigr[:, bass.ds(i * TILE, TILE)], m.bigr[:, bass.ds(i * TILE + 8 * TILE, TILE)], o, d,
                      "ff_read")
        s.last["o"] = lo

    def head(i, previous):
        e_q, c = project(i)
        if previous is not None:
            attend(previous, s.last["vtok_ready"])
        e = values_and_gate(i)
        s.last["vtok_ready"] = to_tokens(s, vtok, vt, e, A(s, 3), "vtok")
        s.last["vt"] = s.last["vtok_ready"]
        levels(e_q, c)

    attend_banks_free(s)
    head(0, None)
    s.loop(KD - 1, lambda i: head(i + 1, i))
    s.last[("a", 2)] = s.last[("a", 1)]
    attend(KD - 1, s.last["vtok_ready"])
    s.last["o_out"] = s.last["o"]


MLA_SIZE = 192


def rope_tables(s):
    m = s.m
    cos, sin = m.big[:, 18 * TILE:19 * TILE], m.big[:, 19 * TILE:20 * TILE]
    ang, k = m.big[:, 16 * TILE:17 * TILE], m.big[:, 17 * TILE:18 * TILE]
    pos = cos.bitcast(I32)
    R = slice(0, 64)
    two_pi = 2 * np.pi
    c1 = float(np.float32(6.28125))
    c2 = float(np.float32(np.round((two_pi - c1) * 2 ** 21) / 2 ** 21))
    c3 = float(np.float32(two_pi - c1 - c2))
    magic = 12582912.0
    s.wait_value(s.dve, m.s_pos, 16, 0)
    d = s.done(s.dve.tensor_copy(ang[R, :], pos[R, :]), "dve")
    s.wait(s.dve, d)
    d = s.done(s.dve.tensor_scalar(ang[R, :], ang[R, :], m.par[R, COL["inv_freq"]:COL["inv_freq"] + 1], None,
                                   ALU.mult), "dve")
    s.wait(s.dve, d)
    d = s.done(s.dve.tensor_scalar(k[R, :], ang[R, :], float(np.float32(1 / two_pi)), magic, ALU.mult, ALU.add), "dve")
    s.wait(s.dve, d)
    d = s.done(s.dve.tensor_scalar(k[R, :], k[R, :], magic, None, ALU.subtract), "dve")
    for c in (c1, c2, c3):
        s.wait(s.dve, d)
        d = s.done(s.dve.scalar_tensor_tensor(out=ang[R, :], in0=k[R, :], scalar=-c, in1=ang[R, :], op0=ALU.mult,
                                              op1=ALU.add), "dve")
    s.wait(s.dve, d)
    lim = 3.1415925
    d = s.done(s.dve.tensor_scalar(ang[R, :], ang[R, :], lim, -lim, ALU.min, ALU.max), "dve")
    s.wait(s.act, d)
    s.done(s.act.activation(sin[R, :], ang[R, :], ACT.Sin), "act")
    e = s.done(s.act.activation(cos[R, :], ang[R, :], ACT.Sin, scale=0.5), "act")
    s.wait(s.dve, e)
    d = s.done(s.dve.tensor_tensor(cos[R, :], cos[R, :], cos[R, :], ALU.mult), "dve")
    s.wait(s.dve, d)
    s.last["rope"] = s.done(s.dve.tensor_scalar(cos[R, :], cos[R, :], -2.0, 1.0, ALU.mult, ALU.add), "dve")


def latent_attention(s):
    m = s.m
    t = lambda k, n=1: m.big[:, k * TILE:(k + n) * TILE]
    cos, sin = t(18), t(19)
    lat_high, lat_low = m.bigr[:, 0:4 * TILE], m.bigr[:, 4 * TILE:8 * TILE]
    R = slice(0, 64)
    kr, krsq = t(0), t(1)

    def rotate(dst, src, mark, bank, tmp):
        s.wait(s.pe, mark, s.last.get(bank[1]))
        mm = s.done(s.pe.matmul(bank[0], m.col("swap", 0, P), src, start=True, stop=True), "pe")
        s.wait(s.dve, mm, s.last["rope"])
        d = s.done(s.dve.tensor_tensor(tmp[R, :], bank[0][R, :], sin[R, :], ALU.mult), "dve")
        s.last[bank[1]] = d
        d2 = s.done(s.dve.tensor_tensor(dst[R, :], src[R, :], cos[R, :], ALU.mult), "dve")
        s.wait(s.dve, d, d2)
        return s.done(s.dve.tensor_tensor(dst[R, :], dst[R, :], tmp[R, :], ALU.add), "dve")

    for j in range(5):
        pe = full_tile(s, j % 4, m.nh, m.nl)
        dst = t(2 + j) if j < 4 else kr
        e = copy_out(s, dst, G(s, j % 4), pe)
        if j < 4:
            add_square(s, dst, j, j % 2 == 0, (e,))
            if j % 2:
                s.wait(s.act, s.last.get("rstd_read"))
                r, _ = make_rstd(s, m.rstd[:, :], 256, A(s, 3))
                for k in (j - 1, j):
                    gain = m.col("g_qa" if j == 1 else "g_kva", k % 2)
                    s.wait(s.dve, r)
                    d = s.done(s.dve.scalar_tensor_tensor(out=t(2 + k), in0=t(2 + k), scalar=gain, in1=m.rstd[:, :],
                                                          op0=ALU.mult, op1=ALU.mult), "dve")
                    sl = slice(k * TILE, (k + 1) * TILE)
                    _, lo = split(s, lat_high[:, sl], lat_low[:, sl], t(2 + k), d, "ff_read")
                s.last["rstd_read"] = d
    s.last["n_read"] = pe
    s.wait(s.act, e)
    sq = s.done(s.act.activation(krsq, kr, ACT.Square), "act")
    s.wait(s.dve, e, sq)
    d = s.done(s.dve.tensor_scalar(kr, kr, m.col("g_k", 1), None, ALU.mult), "dve")
    krot = t(2)
    s.wait(s.dve, lo)
    rot = rotate(krot, kr, d, A(s, 3), t(3))
    s.last["krot"] = rot
    s.wait(s.pe, lo, rot)

    qn, qr, kn, krn, vt, vtok, tmp, qrr = (t(k) for k in (3, 4, 5, 6, 7, 8, 9, 10))
    rq, rk = m.rstd[:, :], t(11)
    sqq, sqk = m.ss[:, :], m.sq[:, 0:TILE]
    sqt = m.sq[:, TILE:2 * TILE]
    probs = [m.big[:, 12 * TILE + o:12 * TILE + o + w] for o, w in ((0, 128), (128, 256), (384, 384), (768, 512))]
    pt = m.big[:, 15 * TILE:15 * TILE + ZW]
    scale = MLA_SIZE ** -0.5
    small = m.small

    def short_tile(bank, blk0):
        base = begin_unit(s)
        s.wait(s.pe, s.last.get(("g", bank)))
        pairs = [(kb, lat_high[:, (blk0 + kb) * TILE:(blk0 + kb + 1) * TILE],
                  lat_low[:, (blk0 + kb) * TILE:(blk0 + kb + 1) * TILE]) for kb in range(2)]
        return end_unit(s, products(s, m.gb(bank), base, pairs))

    def front():
        pes = [short_tile(b, 0 if b < 2 else 2) for b in range(4)]
        s.wait(s.act, pes[1], s.last.get("ss"), s.last.get(("sq", 1)))
        s.done(s.act.activation(sqq, m.gb(0), ACT.Square), "act")
        e = s.done(s.act.activation(sqt, m.gb(1), ACT.Square), "act")
        s.wait(s.dve, e)
        dq = s.done(s.dve.tensor_tensor(sqq, sqq, sqt, ALU.add), "dve")
        s.last[("sq", 1)] = dq
        s.wait(s.act, pes[2], s.last.get(("sq", 0)))
        e = s.done(s.act.activation(sqk, m.gb(2), ACT.Square), "act")
        s.wait(s.dve, e)
        dk = s.done(s.dve.tensor_tensor(sqk, sqk, krsq, ALU.add), "dve")
        e_v = copy_out(s, vt, G(s, 3), pes[3], "vt")
        s.wait(s.act, s.last.get("qk_read"))
        s.done(s.act.activation(qn, m.gb(0), ACT.Copy), "act")
        e1 = s.done(s.act.activation(qr, m.gb(1), ACT.Copy), "act")
        e2 = s.done(s.act.activation(kn, m.gb(2), ACT.Copy), "act")
        for b, e in ((0, e1), (1, e1), (2, e2)):
            s.last[("g", b)] = e
        s.wait(s.act, s.last.get("rstd_read"))
        r, mm = make_rstd(s, rq, MLA_SIZE, G(s, 0), sqq, dq)
        s.last["ss"] = mm
        r2, mm = make_rstd(s, rk, MLA_SIZE, G(s, 1), sqk, dk)
        s.last[("sq", 0)] = mm
        s.wait(s.dve, r, e2)
        dr = s.done(s.dve.scalar_tensor_tensor(out=qr, in0=qr, scalar=m.col("g_q", 1), in1=rq, op0=ALU.mult,
                                               op1=ALU.mult), "dve")
        s.done(s.dve.scalar_tensor_tensor(out=qn, in0=qn, scalar=m.col("g_q", 0), in1=rq, op0=ALU.mult,
                                          op1=ALU.mult), "dve")
        s.wait(s.dve, r2)
        s.done(s.dve.scalar_tensor_tensor(out=kn, in0=kn, scalar=m.col("g_k", 0), in1=rk, op0=ALU.mult,
                                          op1=ALU.mult), "dve")
        s.done(s.dve.tensor_tensor(krn[R, :], krot[R, :], rk[R, :], ALU.mult), "dve")
        d = rotate(qrr, qr, dr, G(s, 2), tmp)
        s.last["rstd_read"] = d
        s.last["front"] = d
        s.last["front_v"] = e_v

    def values_to_tokens():
        s.last["vtok_ready"] = to_tokens(s, vtok, vt, s.last["front_v"], G(s, 3), "vtok")
        s.last["vt"] = s.last["vtok_ready"]

    def scores():
        s.wait(s.pe, s.last["front"])
        marks = []
        for qb in range(TB):
            s.wait(s.pe, s.last.get(("a", qb)))
            n = (qb + 1) * P
            qsl = slice(qb * P, n)
            s.pe.matmul(m.ab(qb, n), qn[:, qsl], kn[:, 0:n], start=True, stop=False, skip_group_check=True)
            s.pe.matmul(m.ab(qb, n), qrr[R, qsl], krn[R, 0:n], start=False, stop=False, skip_group_check=True)
            ins = s.pe.matmul(m.ab(qb, P, qb * P), m.col("ident", 0, P), m.col("mla_mask", 0, P), start=False,
                              stop=True, skip_group_check=True)
            marks.append(s.done(ins, "pe"))
        s.last["qk_read"] = marks[-1]
        return marks

    def softmax(marks):
        mx, nb, sm = (small[:, o:o + TB] for o in (0, 4, 8))
        s.wait(s.dve, s.last.get("mla_small"))
        maxima = []
        for qb in range(TB):
            s.wait(s.dve, marks[qb])
            d = s.done(s.dve.tensor_reduce(mx[:, qb:qb + 1], m.ab(qb, (qb + 1) * P), AX_X, ALU.max), "dve")
            s.wait(s.dve, d)
            maxima.append(s.done(s.dve.tensor_scalar(nb[:, qb:qb + 1], mx[:, qb:qb + 1], -scale, None, ALU.mult), "dve"))
        exps = []
        for qb in range(TB):
            s.wait(s.act, maxima[qb], s.last.get("prob"))
            e = s.done(s.act.activation(probs[qb], m.ab(qb, (qb + 1) * P), ACT.Exp, bias=nb[:, qb:qb + 1],
                                        scale=scale, accum_out=sm[:, qb:qb + 1]), "act")
            s.last[("a", qb)] = e
            exps.append(e)
        s.wait(s.dve, exps[-1])
        d = s.done(s.dve.reciprocal(sm, sm), "dve")
        s.wait(s.dve, d)
        for qb in range(TB):
            d = s.done(s.dve.tensor_scalar(probs[qb], probs[qb], sm[:, qb:qb + 1], None, ALU.mult), "dve")
        s.last["mla_small"] = d
        return d

    def attend(i, d):
        s.wait(s.pe, d, s.last.get(("a", 0)), s.last.get(("a", 1)), s.last.get(("a", 2)))
        for qb in range(TB):
            for kb in range(qb + 1):
                ins = s.pe.transpose(m.ab(0, P, ZOFF[kb] + (qb - kb) * P), probs[qb][:, kb * P:(kb + 1) * P],
                                     m.col("ident", 0, P))
        tr = s.done(ins, "pe")
        s.last["prob"] = tr
        s.wait(s.act, tr, s.last.get("pt"))
        e = s.done(s.act.activation(pt, m.ab(0, ZW), ACT.Copy), "act")
        s.last[("a", 0)] = s.last[("a", 1)] = s.last[("a", 2)] = e
        s.wait(s.pe, e, s.last["vtok_ready"], s.last.get(("a", 3)))
        for kb in range(TB):
            w = S - kb * P
            ins = s.pe.matmul(m.ab(3, w, kb * P), vtok[:, kb * P:(kb + 1) * P], pt[:, ZOFF[kb]:ZOFF[kb] + w],
                              start=kb == 0, stop=kb == 3, skip_group_check=True)
        mm = s.done(ins, "pe")
        s.last["pt"] = s.last["vtok"] = mm
        s.wait(s.act, mm)
        hi = s.done(s.act.activation(m.nh[:, bass.ds(i * TILE, TILE)], m.ab(3), ACT.Copy), "act")
        s.wait(s.dve, hi)
        lo = s.done(s.dve.tensor_tensor(m.nl[:, bass.ds(i * TILE, TILE)], m.ab(3),
                                        m.nh[:, bass.ds(i * TILE, TILE)].bitcast(F32), ALU.subtract), "dve")
        s.last[("a", 3)] = lo
        s.last["mla_out"] = lo

    front()
    values_to_tokens()

    def body(i):
        marks = scores()
        d = softmax(marks)
        front()
        attend(i, d)
        values_to_tokens()
    s.wait(s.act, s.last["n_read"])
    s.loop(KD - 2, body)
    body(KD - 2)
    d = softmax(scores())
    attend(KD - 1, d)
    s.wait(s.pe, s.last["mla_out"])


def second_block(s):
    m = s.m
    pre_norm(s, "g_mix2_0")
    lower_bounds(s)
    recurrence(s)
    s.wait(s.pe, s.last["o_out"])
    project_out(s, m.bigr[:, 0:8 * TILE], m.bigr[:, 8 * TILE:16 * TILE],
                lambda j, ps, pe, key: residual_add(s, j, ps, pe, key))
    s.last["ff_read"] = s.last["n_read"]
    pre_norm(s, "g_ffn2_0")
    conv_feed_forward(s, 0)
    pre_norm(s, "g_mix2_1")
    latent_attention(s)
    project_out(s, m.nh, m.nl, lambda j, ps, pe, key: residual_add(s, j, ps, pe, key))
    s.last["ff_read"] = s.last["n_read"]
    pre_norm(s, "g_ffn2_1")
    conv_feed_forward(s, 1, last=True)


def conv_feed_forward(s, layer, last=False):
    def read_out(group, j, ps, pe, key):
        if group and not last:
            residual_add(s, j, ps, pe, key)
            return
        h = s.m.h[:, j * TILE:(j + 1) * TILE]
        s.wait(s.dve, pe, s.last.get("h"))
        a = s.done(s.dve.tensor_tensor(h, h, ps, ALU.add), "dve")
        s.last[key] = a
        if group:
            s.outputs.append(a)
        elif j == KD - 1:
            s.last["h"] = a
    feed_forward(s, layer, read_out)


def weight_units(w):
    full, short = [], []

    def tile(mat, c, width=P):
        x = mat[:, c:c + width].reshape(-1, P, width).transpose(1, 0, 2)
        return np.pad(x, ((0, 0), (0, 0), (0, P - width))) if width < P else x

    def ffn(w_in, w_down):
        t0 = 0
        for n in GROUPS:
            for j in range(t0, t0 + n):
                full.extend((tile(w_in, j * P), tile(w_in, FF + j * P)))
            for j in range(t0, t0 + n):
                full.append(w_down[j * P:(j + 1) * P].reshape(P, KD, P))
            t0 += n

    w_in, gates = w["w_in"][0], 2304
    full += [tile(w["w_mem_kv"][0], j * P) for j in range(4)]
    full += [tile(w_in, j * P) for j in range(4)]
    full += [tile(w_in, 2048 + j * P) for j in range(2)]
    for u in range(2):
        full.append(np.concatenate([tile(w["w_x_o"][0], (4 * u + k) * P) for k in range(4)], axis=1))
    for i in range(4):
        full += [tile(w_in, 512 * (n + 1) + i * P) for n in range(3)]
        for j in (2 * i, 2 * i + 1):
            full += [tile(w_in, gates + b * D + j * P) for b in (0, 2)]
        full.append(np.concatenate([tile(w["w_pool_o"][0], j * P) for j in (2 * i, 2 * i + 1)], axis=1))
    for j in range(0, KD, 2):
        full += [tile(w_in, gates + D + k * P) for k in (j, j + 1)]
        full.append(np.concatenate([tile(w["w_sb_o"][0], k * P) for k in (j, j + 1)], axis=1))
    full += [tile(w["w_out"][0], j * P) for j in range(KD)]
    ffn(w["w_ffn_in"][0], w["w_ffn_out"][0])
    hgrn = w["hgrn_w_in_2"][0]
    for h in range(KD):
        full += [tile(hgrn, part * D + h * P) for part in (1, 0, 2, 3)]
    full += [tile(w["hgrn_w_out_2"][0], j * P) for j in range(KD)]
    ffn(w["ffn_w_up_2"][0], w["ffn_w_down_2"][0])
    mla = w["mla_w_in_2"][0]
    full += [tile(mla, j * P) for j in range(4)] + [tile(mla, 4 * P, 64)]
    before = len(full)
    for h in range(KD):
        q, kv = w["mla_w_q_up_2"][0], w["mla_w_kv_up_2"][0]
        short += [tile(q, h * MLA_SIZE), tile(q, h * MLA_SIZE + P, 64), tile(kv, h * 2 * P), tile(kv, h * 2 * P + P)]
    full += [tile(w["mla_w_out_2"][0], j * P) for j in range(KD)]
    ffn(w["ffn_w_up_2"][1], w["ffn_w_down_2"][1])
    return full, short, before


def packed(parts, width):
    out = np.empty((len(parts), P, width), np.float32)
    for n, x in enumerate(parts):
        out[n] = x.reshape(P, width)
    return out


def parameters(w):
    par = np.zeros((P, NCOL), np.float32)

    def vec(name, v):
        v = np.asarray(v).reshape(-1)
        n = -(-v.size // P)
        par[:, COL[name]:COL[name] + n] = np.pad(v, (0, n * P - v.size)).reshape(n, P).T

    for name, key in (("g_mix_pre", "norm_mix_pre"), ("g_mem", "norm_mem"), ("pool_scale", "pool_scale"),
                      ("g_mix_post", "norm_mix_post"), ("g_ffn_pre", "norm_ffn_pre"), ("g_ffn_post", "norm_ffn_post"),
                      ("hgrn_lb", "hgrn_lower_bounds_2"), ("g_hgrn_out", "hgrn_out_norm_2"),
                      ("g_qa", "mla_q_a_norm_2"), ("g_kva", "mla_kv_a_norm_2"), ("g_q", "mla_q_norm_2"),
                      ("g_k", "mla_k_norm_2")):
        vec(name, w[key])
    for n in range(2):
        vec(f"g_mix2_{n}", w["norm_mix_2"][n])
        vec(f"g_ffn2_{n}", w["norm_ffn_2"][n])
        vec(f"conv_w{n}", w["ffn_conv_w_2"][n])
        vec(f"conv_b{n}", w["ffn_conv_b_2"][n])

    def mat(name, x):
        par[:x.shape[0], COL[name]:COL[name] + x.shape[1]] = x

    mat("w_mix", w["w_pool_mix"][0].transpose(1, 0, 2).reshape(P, 4 * P))
    r, c = np.arange(P)[:, None], np.arange(P)[None, :]
    mat("ident", r == c)
    mat("ones", np.ones((P, P)))
    mat("neg_tri", -(r >= c).astype(np.float32))
    mat("neg_ones", -np.ones((P, P)))
    mat("sb_mask", np.where(r >= c, NEG, 0.0))
    mat("mla_mask", np.where(c > r, NEG, 0.0))
    levels = [r == c] + [(r // (2 * w) == c // (2 * w)) & (r // w % 2 == 0) & (c // w % 2 == 1) for w in LEVELS]
    mat("levels", np.concatenate(levels, axis=1))
    mat("scan_keep", np.broadcast_to(np.arange(S) % P != 0, (P, S)))
    t = np.arange(16)
    edge = np.concatenate([win / np.minimum(t + 1, win) for win in (2, 4, 8, 16)])
    mat("pool_edge", np.broadcast_to(edge, (P, 64)))
    mat("inv_freq", np.concatenate([INV_FREQ, INV_FREQ])[:, None])
    k, o = np.arange(64)[:, None], np.arange(64)[None, :]
    mat("swap", np.where(k == o - 32, 1.0, 0.0) - np.where(k == o + 32, 1.0, 0.0))
    mat("eps", np.full((P, 1), EPS))
    mat("one", np.ones((P, 1)))
    return par


def feature_tiles(x):
    return np.ascontiguousarray(x.T.reshape(KD, P, x.shape[0]).transpose(1, 0, 2).reshape(P, -1))


N_SHORT = 4 * KD


def run_schedule(nc, ctx, mem, active, real, n_full, before):
    s = Schedule(nc, ctx, mem, active, real)
    s.n_units = n_full + N_SHORT
    s.short = lambda u: before <= u < before + N_SHORT
    s.outputs = []
    for name, owner in (("pe", "pe"), ("act", "act"), ("dve", "dve"), ("hi", "act"), ("use", "pe")):
        if owner == active:
            real.sem_inc(mem.sems[name], Count.START)
    for u in range(HI_LEAD):
        hi_split(s, u)
    first_block(s)
    rope_tables(s)
    second_block(s)
    assert s.unit_a == s.n_units, (s.unit_a, s.n_units)
    return s


def build(nc, n_full, before):
    dram = lambda name, shape, dt=F32, kind="ExternalInput": nc.dram_tensor(name, shape, dt, kind=kind).ap()
    x = dram("x_tiles", (P, KD * TILE))
    memory = dram("memory_tiles", (P, KD * M))
    par = dram("params", (P, NCOL))
    pos = dram("positions", (64, S), I32)
    w_full = dram("weights_full", (n_full, P, UNIT))
    w_short = dram("weights_short", (N_SHORT, P, UNIT_S))
    out = dram("out_tiles", (P, KD * TILE), kind="ExternalOutput")

    with ExitStack() as ctx:
        m = Memory(nc, ctx)
        block = ctx.enter_context(nc.Block())
        outputs = run_schedule(nc, ctx, m, "none", None, n_full, before).outputs
        segments = ((0, before, w_full, 0, UNIT), (before, N_SHORT, w_short, 0, UNIT_S),
                    (before + N_SHORT, n_full - before, w_full, before, UNIT))

        def over_units(eng, body):
            for first, n, src, index, width in segments:
                peel = SLOTS if first == 0 else 0
                rounds = (n - peel) // SLOTS
                for k in range(peel):
                    body(first + k, 0, src, index + k, width)
                with eng.Fori(0, rounds) as i:
                    for k in range(SLOTS):
                        body(first + peel + k, i * SLOTS, src, index + peel + k, width)
                for k in range(peel + rounds * SLOTS, n):
                    body(first + k, 0, src, index + k, width)

        @block.sync
        def _(sp):
            sp.dma_start(m.par[:, :], par).then_inc(m.s_par, 16)
            sp.dma_start(m.big[:, 4 * TILE:8 * TILE], memory).then_inc(m.s_mem, 16)

            def load(u, ahead, src, index, width):
                j = u % SLOTS
                if u >= SLOTS:
                    sp.wait_ge(m.s_lo, ahead + (u - SLOTS + 1))
                sp.dma_start(m.raw[:, j * UNIT:j * UNIT + width], src[bass.ds(ahead + index, 1)]
                             .rearrange("a p n -> (a p) n")).then_inc(m.s_raw[j], 16)
                if u == SLOTS - 1:
                    sp.dma_start(m.h[:, :], x).then_inc(m.s_x, 16)
                    sp.dma_start(m.big[0:64, 18 * TILE:19 * TILE].bitcast(I32), pos).then_inc(m.s_pos, 16)
            over_units(sp, load)
            for j, mark in enumerate(outputs):
                sp.wait_ge(mark.count.sem, mark.a)
                sl = slice(j * TILE, (j + 1) * TILE)
                sp.dma_start(out[:, sl], m.h[:, sl]).then_inc(m.s_out, 16)
            sp.wait_ge(m.s_out, 16 * KD)

        @block.gpsimd
        def _(pool):
            def low(u, ahead, src, index, width):
                j = u % SLOTS
                pool.wait_ge(m.sems["hi"], ahead + (Count.START + u + 1))
                sl = slice(j * UNIT, j * UNIT + width)
                pool.tensor_tensor(m.wl[:, sl], m.raw[:, sl], m.wh[:, sl].bitcast(F32), ALU.subtract)\
                    .then_inc(m.s_lo, 1)
            over_units(pool, low)

        @block.scalar
        def _(act):
            run_schedule(nc, ctx, m, "act", act, n_full, before)

        @block.vector
        def _(dve):
            run_schedule(nc, ctx, m, "dve", dve, n_full, before)

        @block.tensor
        def _(pe):
            run_schedule(nc, ctx, m, "pe", pe, n_full, before)


def kernel(**inputs):
    import concourse.bacc as bacc
    from concourse.bass_utils import run_bass_kernel_spmd

    w = {k: np.asarray(v) for k, v in inputs.items()}
    full, short, before = weight_units(w)
    arrays = {
        "x_tiles": feature_tiles(w["x"][0]),
        "memory_tiles": feature_tiles(w["mem"][0]),
        "params": parameters(w),
        "positions": np.ascontiguousarray(np.broadcast_to(w["positions_2"], (64, S))),
        "weights_full": packed(full, UNIT),
        "weights_short": packed(short, UNIT_S),
    }
    nc = bacc.Bacc("TRN2", target_bir_lowering=False, num_devices=1)
    build(nc, len(full), before)
    r = run_bass_kernel_spmd(nc, [arrays], core_ids=[0])
    y = r.results[0]["out_tiles"].reshape(P, KD, S)
    return np.ascontiguousarray(y.transpose(2, 1, 0).reshape(1, S, D))
```

```python
from contextlib import ExitStack

import numpy as np

import concourse.bass as bass
from concourse import mybir

P = 128
S = 512
D = 1024
KD = D // P
M = 256
FF = 2816
NFF = FF // P
GROUPS = (12, NFF - 12)
EPS = 1e-6
NEG = -1.0e30
TB = S // P
TILE = S
BLOCKS = 8
UNIT = BLOCKS * P
UNIT_S = 2 * P
SLOTS = 4
LOGEXP, SIGMOID, SILU, TRIG = "natural_log_exp_and_others", "sigmoid_and_others", "silu_and_others", "trig_and_small"
LEVELS = (64, 32, 16, 8, 4, 2, 1)
ZOFF = (0, 512, 1024, 896)
ZW = 1280
INV_FREQ = (np.float32(10000.0) ** (-np.arange(0, 64, 2, dtype=np.float32) / np.float32(64.0))).astype(np.float32)

F32 = mybir.dt.float32
F32R = mybir.dt.float32r
I32 = mybir.dt.int32
U32 = mybir.dt.uint32
ALU = mybir.AluOpType
ACT = mybir.ActivationFunctionType
AX_X = mybir.AxisListType.X

_COLS = (
    ("g_mix_pre", 8), ("g_mem", 8), ("eps", 1), ("ones", 128), ("ident", 128), ("pool_scale", 4), ("g_mix_post", 8), ("g_ffn_pre", 8), ("g_ffn_post", 8),
    ("g_mix2_0", 8), ("g_mix2_1", 8), ("g_ffn2_0", 8), ("g_ffn2_1", 8), ("hgrn_lb", 8), ("g_hgrn_out", 1),
    ("g_qa", 2), ("g_kva", 2), ("g_q", 2), ("g_k", 2), ("conv_w0", 132), ("conv_b0", 44), ("conv_w1", 132),
    ("conv_b1", 44), ("w_mix", 512), ("neg_tri", 128), ("neg_ones", 128),
    ("sb_mask", 128), ("mla_mask", 128), ("levels", 896), ("scan_keep", 512), ("pool_edge", 64),
    ("inv_freq", 1), ("swap", 128), ("one", 1),
)
COL, NCOL = {}, 0
for _name, _n in _COLS:
    COL[_name] = NCOL
    NCOL += _n
FIRST_COLS = COL["pool_scale"]


class Count:

    START = 96

    def __init__(self, sem):
        self.sem, self.a, self.b = sem, self.START, 0


class Mark:

    def __init__(self, count, a, b):
        self.count, self.a, self.b = count, a, b


def nothing(*args, **kwargs):
    return None


class Absent:

    preload_act_table_set = matmul = transpose = activation = tensor_tensor = tensor_scalar = staticmethod(nothing)
    tensor_copy = memset = copy_predicated = scalar_tensor_tensor = tensor_tensor_scan = staticmethod(nothing)
    tensor_reduce = reciprocal = staticmethod(nothing)


ABSENT = Absent()


class Schedule:
    def __init__(self, nc, ctx, mem, active, real):
        self.nc, self.m = nc, mem
        self.i, self.looping = 0, False
        self.table = None
        self.ready = []
        self.rest = nothing
        self.split_ahead = False
        self.active, self.real = active, real
        self.seen = {}
        self.pe = real if active == "pe" else ABSENT
        self.act = real if active == "act" else ABSENT
        self.dve = real if active == "dve" else ABSENT
        self.c = {n: Count(s) for n, s in mem.sems.items()}
        self.last = {}
        self.unit_a, self.unit_b = 0, 0

    def done(self, ins, name, by=1):
        c = self.c[name]
        if ins is not None:
            ins.then_inc(c.sem, by)
        c.a += by
        return Mark(c, c.a, c.b)

    def wait(self, eng, *marks):
        for mk in marks:
            if mk is not None:
                self.wait_value(eng, mk.count.sem, mk.a, mk.b)

    def wait_value(self, eng, sem, a, b):
        if eng is ABSENT:
            return
        key = id(sem)
        if b and self.looping:
            assert a > 0, "a wait's value stays positive"
            eng.wait_ge(sem, self.i * b + a)
        else:
            if self.seen.get(key, 0) >= a:
                return
            self.seen[key] = a
            eng.wait_ge(sem, a)

    def tables(self, name):
        if self.table != name:
            self.act.preload_act_table_set(name)
            self.table = name

    def loop(self, n, body):
        before = {k: (c.a, c.b) for k, c in self.c.items()}
        unit, last, table = self.unit_a, dict(self.last), self.table
        engines = self.pe, self.act, self.dve
        self.pe = self.act = self.dve = ABSENT
        body(0)
        self.pe, self.act, self.dve = engines
        if self.table != table:
            self.table = None
        step = {k: c.a - before[k][0] for k, c in self.c.items()}
        unit_step = self.unit_a - unit
        assert unit_step % SLOTS == 0
        names = {id(c): k for k, c in self.c.items()}
        carried = {k: mk for k, mk in self.last.items() if mk is not None and last.get(k) is not mk}
        for k, mk in carried.items():
            ahead = last.get(k)
            if ahead is not None and not (ahead.count is mk.count and ahead.a <= mk.a - step[names[id(mk.count)]]):
                for e in engines:
                    self.wait(e, ahead)
        for k, c in self.c.items():
            c.a, c.b = before[k][0], step[k]
        self.unit_a, self.unit_b = unit, unit_step
        self.last = dict(last)
        for k, mk in carried.items():
            st = step[names[id(mk.count)]]
            self.last[k] = Mark(mk.count, mk.a - st, st)
        self.looping = True
        if self.real is None:
            body(0)
        else:
            with self.real.Fori(0, n) as i:
                self.i = i
                body(i)
        self.looping, self.i = False, 0
        for k, c in self.c.items():
            c.a, c.b = before[k][0] + n * step[k], 0
        self.unit_a, self.unit_b = unit + n * unit_step, 0
        for k, mk in self.last.items():
            if mk is not None and mk.b:
                self.last[k] = Mark(mk.count, mk.a + (n - 1) * mk.b, 0)


class Memory:

    def __init__(self, nc, ctx):
        sb = lambda n, w, d=F32: ctx.enter_context(nc.sbuf_tensor(n, [P, w], d))
        self.raw = sb("weights_raw", SLOTS * UNIT)
        self.wh = sb("weights_high", SLOTS * UNIT, F32R)
        self.wl = sb("weights_low", SLOTS * UNIT, F32R)
        self.h = sb("residual", KD * TILE)
        self.nh = sb("normed_high", KD * TILE, F32R)
        self.nl = sb("normed_low", KD * TILE, F32R)
        self.par = sb("parameters", NCOL)
        self.big = sb("scratch", 20 * TILE)
        self.bigr = sb("operands_high_low", 2 * 12 * TILE, F32R)
        self.ss = sb("sum_of_squares", TILE)
        self.sq = sb("squares", 2 * TILE)
        self.rstd = sb("rstd", TILE)
        self.rstd2 = self.big[:, 19 * TILE:20 * TILE]
        self.small = sb("small", 64)
        self.g_bank = ctx.enter_context(nc.psum_tensor("ps_gemm", [P, 4 * 512], F32))
        self.a_bank = ctx.enter_context(nc.psum_tensor("ps_attend", [P, 4 * 512], F32))
        names = ("pe", "act", "dve", "hi", "use")
        self.sems = {n: ctx.enter_context(nc.semaphore(f"s_{n}")) for n in names}
        self.s_lo = ctx.enter_context(nc.semaphore("s_weights_low"))
        self.s_raw = [ctx.enter_context(nc.semaphore(f"s_raw{j}")) for j in range(SLOTS)]
        self.s_gains = ctx.enter_context(nc.semaphore("s_first_parameters"))
        self.s_par = ctx.enter_context(nc.semaphore("s_parameters"))
        self.s_x = ctx.enter_context(nc.semaphore("s_x"))
        self.s_pos = ctx.enter_context(nc.semaphore("s_positions"))
        self.s_mem = ctx.enter_context(nc.semaphore("s_memory_input"))
        self.s_out = ctx.enter_context(nc.semaphore("s_outputs"))

    def col(self, name, k=0, n=1):
        c = COL[name]
        return self.par[:, bass.ds(k + c, n)] if not isinstance(k, int) else self.par[:, c + k:c + k + n]

    def gb(self, b, w=512, off=0):
        return self.g_bank[:, b * 512 + off:b * 512 + off + w]

    def ab(self, b, w=512, off=0):
        return self.a_bank[:, b * 512 + off:b * 512 + off + w]


HI_LEAD = 3


def hi_split(s, lead=HI_LEAD):
    m, act = s.m, s.act
    u, ub = s.unit_a + lead, s.unit_b
    if u >= s.n_units:
        return
    j = u % SLOTS
    w = UNIT_S if s.short(u) else UNIT
    s.wait_value(act, m.s_raw[j], 16 * (u // SLOTS + 1), 16 * (ub // SLOTS))
    s.wait_value(act, s.c["use"].sem, Count.START + u - SLOTS + 1, ub)
    ins = act.activation(m.wh[:, j * UNIT:j * UNIT + w], m.raw[:, j * UNIT:j * UNIT + w], ACT.Copy)
    s.done(ins, "hi")


def begin_unit(s):
    if s.split_ahead:
        s.split_ahead = False
    else:
        hi_split(s)
    return begin_unit_after(s, 0)


def begin_unit_after(s, n):
    u, ub = s.unit_a + n, s.unit_b
    s.wait_value(s.pe, s.c["hi"].sem, Count.START + u + 1, ub)
    s.wait_value(s.pe, s.m.s_lo, u + 1, ub)
    return (u % SLOTS) * UNIT


def end_unit(s, ins):
    s.unit_a += 1
    return s.done(ins, "use")


def products(s, out, base, pairs, start=True, stop=True):
    m, ins = s.m, None
    for n, (blk, xh, xl) in enumerate(pairs):
        c = base + blk * P
        for k, (w, x) in enumerate(((m.wh, xh), (m.wl, xh), (m.wh, xl))):
            ins = s.pe.matmul(out, w[:, c:c + P], x, start=start and n == 0 and k == 0,
                              stop=stop and n == len(pairs) - 1 and k == 2, skip_group_check=True)
    return ins


def full_tile(s, bank, xh, xl, width=TILE):
    if s.ready:
        return s.ready.pop(0)
    for pe in tile_quarters(s, bank, xh, xl, width):
        pass
    return pe


def tile_quarters(s, bank, xh, xl, width=TILE):
    base = begin_unit(s)
    s.wait(s.pe, s.last.get(("g", bank)))
    pairs = [(kb, xh[:, kb * width:(kb + 1) * width], xl[:, kb * width:(kb + 1) * width]) for kb in range(KD)]
    for k in range(0, KD, 2):
        ins = products(s, s.m.gb(bank, width), base, pairs[k:k + 2], start=k == 0, stop=k == KD - 2)
        yield end_unit(s, ins) if k == KD - 2 else None


def add_square(s, src, j, first, marks, width=TILE):
    m = s.m
    sl = m.sq[:, (j % 2) * TILE:(j % 2) * TILE + width]
    s.wait(s.act, *marks)
    if first:
        s.wait(s.act, s.last.get("ss"))
        sq = s.done(s.act.activation(m.ss[:, 0:width], src, ACT.Square), "act")
        s.last["ss_sum"] = sq
        return nothing
    s.wait(s.act, s.last.get(("sq", j % 2)))
    sq = s.done(s.act.activation(sl, src, ACT.Square), "act")

    def add():
        s.wait(s.dve, sq, s.last["ss_sum"])
        su = s.done(s.dve.tensor_tensor(m.ss[:, 0:width], m.ss[:, 0:width], sl, ALU.add), "dve")
        s.last[("sq", j % 2)] = su
        s.last["ss_sum"] = su
    return add


def make_rstd(s, out, size, bank, ss=None, ss_mark=None, width=TILE):
    m = s.m
    own = ss is None
    ss = m.ss[:, 0:width] if own else ss
    ps = bank[0][:, 0:width]
    s.wait(s.pe, s.last["ss_sum"] if own else ss_mark, s.last.get(bank[1]))
    mm = s.done(s.pe.matmul(ps, m.col("ones", 0, P), ss, start=True, stop=True), "pe")
    if own:
        s.last["ss"] = mm
    s.tables(LOGEXP)
    s.wait(s.act, mm)
    ln = s.done(s.act.activation(out, ps, ACT.Ln, bias=m.col("eps"), scale=1.0 / size), "act")
    s.last[bank[1]] = ln
    s.wait(s.act, ln)
    return s.done(s.act.activation(out, out, ACT.Exp, scale=-0.5), "act"), mm


def split(s, high, low, src, mark, key=None):
    s.wait(s.act, mark, s.last.get(key) if key else None)
    hi = s.done(s.act.activation(high, src, ACT.Copy), "act")
    s.wait(s.dve, hi, mark)
    lo = s.done(s.dve.tensor_tensor(low, src, high.bitcast(F32), ALU.subtract), "dve")
    return hi, lo


def operand_tile(s, gain, j, marks):
    m = s.m
    sl = slice(j * TILE, (j + 1) * TILE)
    return make_operand(s, m.h[:, sl], m.nh[:, sl], m.nl[:, sl], m.col(gain, j), j, marks + (s.last.get("n_read"),))


def make_operand(s, src, hi, lo, gain, j, marks, width=TILE):
    s.wait(s.act, *marks)
    a = s.done(s.act.activation(hi, src, ACT.Identity, scale=gain), "act")
    add = add_square(s, src, j, j == 0, marks, width)

    def rest():
        s.wait(s.dve, a)
        s.last[("n", j)] = s.done(s.dve.scalar_tensor_tensor(out=lo, in0=src, scalar=gain, in1=hi.bitcast(F32),
                                                             op0=ALU.mult, op1=ALU.subtract), "dve")
        add()
    return rest


WIDE = 3


def wide_tiles(s, xh, xl, mark):
    m = s.m
    bases = [begin_unit(s)] + [begin_unit_after(s, n) for n in range(1, WIDE)]
    for b in range(WIDE):
        s.wait(s.pe, s.last.get(("g", b)))
    for kb in range(KD):
        sl = slice(kb * TILE, (kb + 1) * TILE)
        s.wait(s.pe, mark(kb))
        for b, base in enumerate(bases):
            ins = products(s, m.gb(b), base, [(kb, xh[:, sl], xl[:, sl])], start=kb == 0, stop=kb == KD - 1)
            if kb == KD - 1:
                s.ready.append(end_unit(s, ins))
        if kb == KD - 1:
            for n in range(WIDE):
                hi_split(s, HI_LEAD - WIDE + 1 + n)
            s.split_ahead = True
        yield


def wide_start(s):
    for _ in wide_tiles(s, s.m.nh, s.m.nl, lambda kb: s.last[("n", kb)]):
        pass
    s.wait(s.act, s.last.get("rstd_read"))
    s.last["rstd"], _ = make_rstd(s, s.m.rstd[:, :], D, A(s, 3))


def scaled(s, dst, ps, pe, key, scale=1.0, free=None):
    s.wait(s.dve, pe, s.last["rstd"], s.last.get(free) if free else None)
    rstd = s.m.rstd[:, 0:dst.shape[1]]
    if scale == 1.0:
        ins = s.dve.tensor_tensor(dst, ps, rstd, ALU.mult)
    else:
        ins = s.dve.scalar_tensor_tensor(out=dst, in0=ps, scalar=scale, in1=rstd, op0=ALU.mult, op1=ALU.mult)
    d = s.done(ins, "dve")
    s.last[key] = d
    s.last["rstd_read"] = d
    return d


def A(s, k):
    return (s.m.ab(k), ("a", k))


def G(s, k):
    return (s.m.gb(k), ("g", k))


def attend_banks_free(s):
    s.wait(s.pe, *(s.last.get(("a", k)) for k in range(4)))


def project_out(s, xh, xl, into):
    for j in range(KD):
        pe = full_tile(s, j % 4, xh, xl)
        into(j, s.m.gb(j % 4), pe, ("g", j % 4))
    s.last["n_read"] = pe


def residual_add(s, j, ps, pe, key, gain):
    m = s.m
    h = m.h[:, j * TILE:(j + 1) * TILE]
    s.wait(s.dve, pe, s.last.get("h"))
    a = s.done(s.dve.tensor_tensor(h, h, ps, ALU.add), "dve")
    s.last[key] = a
    before, s.rest = s.rest, operand_tile(s, gain, j, (a,))
    before()
    if j == KD - 1:
        s.rest()
        s.rest = nothing


def keep_branch(s, j, ps, pe, key, acc=None):
    m = s.m
    f = m.big[:, j * TILE:(j + 1) * TILE]
    if acc is None:
        s.wait(s.act, pe, s.last.get("f"))
        a = s.done(s.act.activation(f, ps, ACT.Copy), "act")
    else:
        s.wait(s.dve, pe, acc)
        a = s.done(s.dve.tensor_tensor(f, f, ps, ALU.add), "dve")
    s.last[key] = a
    add_square(s, f, j, j == 0, (a,))()
    return a


def post_norm_add(s, gain, next_gain):
    m = s.m
    s.wait(s.act, s.last.get("rstd2_read"))
    r, _ = make_rstd(s, m.rstd2, D, A(s, 3))
    rest = nothing
    for j in range(KD):
        sl = slice(j * TILE, (j + 1) * TILE)
        f, h = m.big[:, sl], m.h[:, sl]
        s.wait(s.dve, r)
        a = s.done(s.dve.scalar_tensor_tensor(out=f, in0=f, scalar=m.col(gain, j), in1=m.rstd2, op0=ALU.mult,
                                              op1=ALU.mult), "dve")
        s.last["rstd2_read"] = a
        s.wait(s.dve, a)
        a = s.done(s.dve.tensor_tensor(h, h, f, ALU.add), "dve")
        s.last["f"] = a
        before, rest = rest, operand_tile(s, next_gain, j, (a,))
        before()
    rest()


def feed_forward(s, conv, read_out, split_at, during=None):
    m = s.m
    y = [m.big[:, (8 + k) * TILE:(9 + k) * TILE] for k in range(4)]
    tile0 = 0
    wide_start(s)
    for group, n in enumerate(GROUPS):
        def up_pair(k, idx):
            for half in range(2):
                b = 2 * k + half
                pe = full_tile(s, b, m.nh, m.nl)
                ps, out = m.gb(b), y[b]
                if conv is None:
                    d = scaled(s, out, ps, pe, ("g", b), free=("y", b))
                    if half == 0:
                        s.wait(s.act, d)
                        gate = s.done(s.act.activation(out, out, ACT.Silu), "act")
                    else:
                        t = y[2 * k]
                        s.wait(s.dve, d, gate)
                        prod = s.done(s.dve.tensor_tensor(t, t, out, ALU.mult), "dve")
                else:
                    c = 22 * half + tile0
                    w = lambda tap: m.col(f"conv_w{conv}", idx + (44 * tap + c))
                    u = (m.sq[:, 0:TILE], m.sq[:, TILE:2 * TILE])[half]
                    d = scaled(s, u, ps, pe, ("g", b), free=("sq", half))
                    s.wait(s.act, d, s.last.get(("y", b)))
                    e = s.done(s.act.activation(out, u, ACT.Identity, bias=m.col(f"conv_b{conv}", idx + c),
                                                scale=w(2)), "act")
                    s.wait(s.dve, e)
                    e = s.done(s.dve.scalar_tensor_tensor(out=out[:, 1:S], in0=u[:, 0:S - 1], scalar=w(1),
                                                          in1=out[:, 1:S], op0=ALU.mult, op1=ALU.add), "dve")
                    s.wait(s.dve, e)
                    e = s.done(s.dve.scalar_tensor_tensor(out=out[:, 2:S], in0=u[:, 0:S - 2], scalar=w(0),
                                                          in1=out[:, 2:S], op0=ALU.mult, op1=ALU.add), "dve")
                    s.last[("sq", half)] = e
                    if half == 0:
                        s.wait(s.act, e)
                        gate = s.done(s.act.activation(out, out, ACT.Silu), "act")
                    else:
                        s.wait(s.dve, gate, e)
                        prod = s.done(s.dve.tensor_tensor(y[2 * k], y[2 * k], out, ALU.mult), "dve")
                        s.last[("y", b)] = prod
            cols = bass.ds(idx * TILE, TILE)
            low = bass.ds(idx * TILE + 12 * TILE, TILE)
            _, lo = split(s, m.bigr[:, cols], m.bigr[:, low], y[2 * k], prod, "ff_read")
            s.last[("y", 2 * k)] = lo
            s.last["ff_before"], s.last["ff"] = s.last.get("ff"), lo

        def up_body(i):
            for k in range(2):
                up_pair(k, i * 2 + k)
        s.tables(SILU)
        up_body(0)
        s.loop(n // 2 - 1, lambda i: up_body(i + 1))
        s.wait(s.pe, s.last["ff_before"])
        if group:
            s.tables(LOGEXP)

        def operand(idx):
            return m.bigr[:, bass.ds(idx * TILE, TILE)], m.bigr[:, bass.ds(idx * TILE + 12 * TILE, TILE)]

        def down_unit(idx, open_bank=False):
            base = begin_unit(s)
            xh, xl = operand(idx)
            for b in range(KD):
                ps, key = G(s, b) if b < 4 else A(s, b - 4)
                if open_bank:
                    s.wait(s.pe, s.last.get(key))
                ins = products(s, ps, base, [(b, xh, xl)], start=open_bank, stop=False)
            return end_unit(s, ins)

        def last_units():
            bases = begin_unit(s), begin_unit_after(s, 1)
            marks = []
            for b in range(KD):
                ps, _ = G(s, b) if b < 4 else A(s, b - 4)
                ins = [products(s, ps, bases[k], [(b, *operand(n - 2 + k))], start=False, stop=k == 1)
                       for k in range(2)]
                if b < KD - 1:
                    marks.append(s.done(ins[1], "pe"))
            end_unit(s, ins[0])
            marks.append(end_unit(s, ins[1]))
            return marks

        def down_body(i):
            for k in range(4):
                down_unit(i * 4 + (k + 1))
        down_unit(0, open_bank=True)
        rounds = (n - 3) // 4
        s.loop(rounds, down_body)
        if group == 0 and during:
            during()
        for k in range(4 * rounds + 1, n - 2):
            down_unit(k)
        s.wait(s.pe, s.last["ff"])
        marks = last_units()
        s.last["ff_read"] = marks[-1]
        for j in range(KD):
            if j == split_at:
                hi_split(s, HI_LEAD - 1)
            ps, key = (G(s, j) if j < 4 else A(s, j - 4))
            read_out(group, j, ps, marks[j], key)
        tile0 += n
    s.last["n_read"] = s.last["ff_read"]


def to_tokens(s, dst, src, mark, bank, key):
    m, nb = s.m, src.shape[1] // P
    s.wait(s.pe, mark, s.last.get(bank[1]))
    for b in range(nb):
        ins = s.pe.transpose(bank[0][:, b * P:(b + 1) * P], src[:, b * P:(b + 1) * P], m.col("ident", 0, P))
    t = s.done(ins, "pe")
    s.wait(s.act, t, s.last.get(key))
    e = s.done(s.act.activation(dst, bank[0][:, 0:nb * P], ACT.Copy), "act")
    s.last[bank[1]] = e
    return e


def copy_out(s, dst, bank, pe, key=None, scale=1.0):
    s.wait(s.act, pe, s.last.get(key) if key else None)
    e = s.done(s.act.activation(dst, bank[0][:, 0:dst.shape[1]], ACT.Copy, scale=scale), "act")
    s.last[bank[1]] = e
    return e


def memory_products(s):
    m = s.m
    mem = m.big[:, 4 * TILE:8 * TILE]
    s.tables(LOGEXP)
    for e in (s.act, s.dve, s.pe):
        s.wait_value(e, m.s_gains, 16, 0)
    s.wait_value(s.act, m.s_mem, 16, 0)
    s.wait_value(s.dve, m.s_mem, 16, 0)
    high, low = m.bigr[:, 0:KD * M], m.bigr[:, KD * M:2 * KD * M]
    rest = nothing
    for j in range(KD):
        sl = slice(j * M, (j + 1) * M)
        before, rest = rest, make_operand(s, mem[:, sl], high[:, sl], low[:, sl], m.col("g_mem", j), j, (), M)
        before()
        if j % 2 and j // 2 < HI_LEAD:
            hi_split(s, j // 2)
    rest()
    for j in range(4):
        base = begin_unit(s)
        for kb in range(KD):
            s.wait(s.pe, s.last[("n", kb)])
            sl = slice(kb * M, (kb + 1) * M)
            ins = products(s, m.ab(j // 2, M, (j % 2) * M), base, [(kb, high[:, sl], low[:, sl])],
                           start=kb == 0 and j % 2 == 0, stop=kb == KD - 1)
        pe = end_unit(s, ins)
    s.last["mem_read"] = pe
    s.last["mem_rstd"], _ = make_rstd(s, m.rstd2[:, 0:M], D, A(s, 3), width=M)


def memory_values(s):
    m = s.m
    s.wait(s.dve, s.last["mem_rstd"], s.last["mem_read"])
    for j in range(4):
        d = s.done(s.dve.tensor_tensor(m.big[:, j * M:(j + 1) * M], m.ab(j // 2, M, (j % 2) * M), m.rstd2[:, 0:M],
                                       ALU.mult), "dve")
    s.last["mem_kv"] = s.last[("a", 0)] = s.last[("a", 1)] = s.last["rstd2_read"] = d
    for j in range(2):
        s.last["mem_vals"] = to_tokens(s, m.big[:, (4 + j) * M:(5 + j) * M], m.big[:, (2 + j) * M:(3 + j) * M],
                                       s.last["mem_kv"], A(s, 2), None)


def pool_bank(g):
    return (g + 2) % 4


def pool_group(s, g, pe):
    m, bank = s.m, pool_bank(g)
    p, a, b = m.big[:, 16 * TILE:17 * TILE], m.big[:, 17 * TILE:18 * TILE], m.rstd2
    src, dst, last = p, a, scaled(s, p, m.gb(bank), pe, ("g", bank))
    for k in range(g + 1):
        w = 1 << k
        s.wait(s.dve, last, s.last.get("pool_ab"), s.last.get("pool_out"))
        s.done(s.dve.tensor_copy(dst[:, 0:w], src[:, 0:w]), "dve")
        last = s.done(s.dve.tensor_tensor(dst[:, w:S], src[:, w:S], src[:, 0:S - w], ALU.add), "dve")
        src, dst = dst, (b if dst is a else a)
    s.wait(s.dve, last)
    edge = s.done(s.dve.tensor_tensor(src[:, 0:16], src[:, 0:16], m.col("pool_edge", 16 * g, 16), ALU.mult), "dve")
    s.wait(s.dve, edge)
    mix = s.done(s.dve.scalar_tensor_tensor(out=src, in0=src, scalar=1.0 / (2 << g), in1=p, op0=ALU.mult,
                                            op1=ALU.subtract), "dve")

    def finish():
        s.wait(s.pe, mix, s.last.get(("g", bank)))
        mm = s.done(s.pe.matmul(m.gb(bank), m.col("w_mix", g * P, P), src, start=True, stop=True), "pe")
        s.last["pool_ab"] = mm
        s.wait(s.act, mm)
        y = s.done(s.act.activation(dst, m.gb(bank), ACT.Identity, scale=m.col("pool_scale", g)), "act")
        s.last[("g", bank)] = y
        o = (2 * KD * M) + g * TILE
        _, lo = split(s, m.bigr[:, o:o + TILE], m.bigr[:, o + 4 * TILE:o + 5 * TILE], dst, y)
        s.last["pool_out"] = s.last["rstd2_read"] = lo
    return finish


def memory_attention(s):
    m = s.m
    keys, vals = m.big[:, 0:2 * M], m.big[:, 4 * M:6 * M]
    xq = m.big[:, 4 * TILE:6 * TILE]
    prob = m.big[:, 6 * TILE:8 * TILE]
    pt = m.big[:, 8 * TILE:16 * TILE]
    for e in (s.act, s.dve, s.pe):
        s.wait_value(e, m.s_par, 16, 0)
    for j in range(2):
        pe = full_tile(s, j, m.nh, m.nl)
        e = scaled(s, xq[:, j * TILE:(j + 1) * TILE], m.gb(j), pe, ("g", j))
    s.wait(s.pe, e, s.last["mem_kv"])
    mx, nb, sm = m.small[:, 0:4], m.small[:, 4:8], m.small[:, 8:12]
    pool_pe, pool_end = full_tile(s, pool_bank(0), m.nh, m.nl), nothing
    for tb in range(TB):
        s.wait(s.pe, s.last.get(("a", 0)), s.last.get(("a", 1)))
        for h in range(4):
            r, tile = 64 * (h % 2), h // 2
            out = m.ab(h % 2, M, (h // 2) * M)
            ins = s.pe.matmul(out, xq[r:r + 64, tile * TILE + tb * P:tile * TILE + (tb + 1) * P],
                              keys[r:r + 64, tile * M:(tile + 1) * M], start=h < 2, stop=h >= 2, skip_group_check=True)
        mm = s.done(ins, "pe")
        s.wait(s.dve, mm, s.last.get("x_small"))
        sc = m.a_bank[:, 0:4 * M].rearrange("p (h m) -> p h m", h=4)
        d = s.done(s.dve.tensor_reduce(mx, sc, AX_X, ALU.max), "dve")
        s.wait(s.dve, d)
        d = s.done(s.dve.tensor_scalar(nb, mx, -0.125, None, ALU.mult), "dve")
        s.wait(s.act, d, s.last.get("prob"))
        for h in range(4):
            e = s.done(s.act.activation(prob[:, h * M:(h + 1) * M], m.a_bank[:, h * M:(h + 1) * M], ACT.Exp,
                                        bias=nb[:, h:h + 1], scale=0.125, accum_out=sm[:, h:h + 1]), "act")
        s.last[("a", 0)] = s.last[("a", 1)] = e
        s.wait(s.dve, e)
        d = s.done(s.dve.reciprocal(sm, sm), "dve")
        s.wait(s.dve, d)
        for h in range(4):
            d = s.done(s.dve.tensor_scalar(prob[:, h * M:(h + 1) * M], prob[:, h * M:(h + 1) * M],
                                           sm[:, h:h + 1], None, ALU.mult), "dve")
        s.last["x_small"] = d
        group_pe = pool_pe
        if tb < TB - 1:
            pool_pe = full_tile(s, pool_bank(tb + 1), m.nh, m.nl)
        pool_end()
        pool_end = pool_group(s, tb, group_pe)
        s.wait(s.pe, d, s.last.get(("a", 2)), s.last.get(("a", 3)))
        for k in range(8):
            ins = s.pe.transpose(m.ab(2 + k // 4, P, (k % 4) * P), prob[:, k * P:(k + 1) * P], m.col("ident", 0, P))
        t = s.done(ins, "pe")
        s.last["prob"] = t
        s.wait(s.act, t)
        dst = pt.rearrange("p (k t) -> p k t", k=8)[:, :, tb * P:(tb + 1) * P]
        e = s.done(s.act.activation(dst, m.a_bank[:, 1024:2048].rearrange("p (k t) -> p k t", k=8), ACT.Copy), "act")
        s.last[("a", 2)] = s.last[("a", 3)] = e
    s.wait(s.pe, e)
    for j in range(2):
        s.wait(s.pe, s.last.get(("a", j)))
        for h in (2 * j, 2 * j + 1):
            k = (h % 2) * 2 + h // 2
            r = 64 * (h % 2)
            for mb in range(2):
                ins = s.pe.matmul(m.a_bank[r:r + 64, j * 512:(j + 1) * 512],
                                  vals[:, j * M + mb * P + r:j * M + mb * P + r + 64],
                                  pt[:, (2 * k + mb) * TILE:(2 * k + mb + 1) * TILE], start=mb == 0, stop=mb == 1,
                                  skip_group_check=True)
        mm = s.done(ins, "pe")
        s.wait(s.act, s.last["mem_read"])
        _, lo = split(s, m.bigr[:, j * TILE:(j + 1) * TILE], m.bigr[:, (2 + j) * TILE:(3 + j) * TILE], m.ab(j), mm)
        s.last[("a", j)] = lo
    s.last["x_out"] = lo
    pool_end()


def cross_branch_out(s):
    m = s.m
    y = m.big[:, 0:KD * TILE]
    s.wait(s.pe, s.last["x_out"])
    for u in range(2):
        base = begin_unit(s)
        for k in range(4):
            s.wait(s.pe, s.last.get(("g", k)))
            pairs = [(2 * k + kb, m.bigr[:, kb * TILE:(kb + 1) * TILE], m.bigr[:, (2 + kb) * TILE:(3 + kb) * TILE])
                     for kb in range(2)]
            ins = products(s, m.gb(k), base, pairs)
            if k < 3:
                pe = s.done(ins, "pe")
            else:
                pe = end_unit(s, ins)
            j = 4 * u + k
            s.last["merged"] = copy_out(s, y[:, j * TILE:(j + 1) * TILE], G(s, k), pe)
    s.last["x_read"] = pe


def stick_breaking(s):
    m = s.m
    c0 = KD * TILE
    q, k, vt = (m.big[:, c0 + n * TILE:c0 + (n + 1) * TILE] for n in range(3))
    vtok = m.big[:, c0 + 3 * TILE:c0 + 4 * TILE]
    c1 = c0 + 4 * TILE
    lg = [m.big[:, c1 + n * ZW:c1 + (n + 1) * ZW] for n in range(2)]
    gate = [m.sq[:, 0:TILE], m.sq[:, TILE:2 * TILE]]
    at = m.ss[:, :]
    zb = m.a_bank[:, 0:ZW]
    o_high, o_low = 2 * KD * M + 8 * TILE, 2 * KD * M + 12 * TILE

    def body(i):
        for n, (dst, scale) in enumerate(((q, 0.125), (k, 1.0), (vt, 1.0))):
            pe = full_tile(s, n, m.nh, m.nl)
            e = scaled(s, dst, m.gb(n), pe, ("g", n), scale, ("sb", n))
        e_v = to_tokens(s, vtok, vt, e, A(s, 3), "vtok")
        s.last[("sb", 2)] = e_v

        def scores(hh):
            r = 64 * hh
            s.wait(s.pe, e, s.last.get(("a", 0)))
            for kb in (0, 1, 3, 2):
                w = S - kb * P
                s.pe.matmul(zb[:, ZOFF[kb]:ZOFF[kb] + w], k[r:r + 64, kb * P:(kb + 1) * P], q[r:r + 64, kb * P:S],
                            start=kb != 3, stop=False, skip_group_check=True)
            for kb in range(TB):
                ins = s.pe.matmul(zb[:, ZOFF[kb]:ZOFF[kb] + P], m.col("ident", 0, P), m.col("sb_mask", 0, P),
                                  start=False, stop=False, skip_group_check=True)
            return s.done(ins, "pe")

        def softplus(hh, mm):
            x = lg[hh]
            s.wait(s.act, mm, s.last.get(("lg", hh)))
            s.tables(LOGEXP)
            e0 = s.done(s.act.activation(x, zb, ACT.Abs), "act")
            s.wait(s.act, e0)
            e1 = s.done(s.act.activation(x, x, ACT.Exp, scale=-1.0), "act")
            s.wait(s.act, e1)
            e2 = s.done(s.act.activation(x, x, ACT.Ln, bias=m.col("one")), "act")
            s.wait(s.dve, e2)
            return s.done(s.dve.scalar_tensor_tensor(out=x, in0=zb, scalar=0.0, in1=x, op0=ALU.max, op1=ALU.add), "dve")

        def suffix(hh, d):
            x = lg[hh]
            s.wait(s.pe, d)
            for kb in range(TB):
                for j in range(kb, TB):
                    lhs = m.col("neg_tri" if j == kb else "neg_ones", 0, P)
                    o = ZOFF[kb] + (j - kb) * P
                    ins = s.pe.matmul(zb[:, o:o + S - j * P], lhs, x[:, ZOFF[j]:ZOFF[j] + S - j * P], start=False,
                                      stop=False, skip_group_check=True)
            mm = s.done(ins, "pe")
            s.tables(LOGEXP)
            s.wait(s.act, mm)
            e3 = s.done(s.act.activation(x, zb, ACT.Exp), "act")
            s.last[("a", 0)] = e3
            return e3

        def values(hh, e3):
            r = 64 * hh
            x = lg[hh]
            s.wait(s.pe, e3, e_v, s.last.get(("a", 3)))
            for kb in range(TB):
                ins = s.pe.matmul(m.a_bank[r:r + 64, 3 * 512 + kb * P:4 * 512], vtok[:, kb * P + r:kb * P + r + 64],
                                  x[:, ZOFF[kb]:ZOFF[kb] + S - kb * P], start=kb == 0, stop=kb == 3,
                                  skip_group_check=True)
            mm = s.done(ins, "pe")
            s.last[("lg", hh)] = mm
            return mm

        def pooled(half, ctx, base):
            g0, d, cols = ctx
            s.wait(s.pe, s.last.get(("g", 2 + half)))
            o = 2 * KD * M
            pairs = [(4 * half + kb, m.bigr[:, o + kb * TILE:o + (kb + 1) * TILE],
                      m.bigr[:, o + (4 + kb) * TILE:o + (5 + kb) * TILE]) for kb in range(4)]
            ins = products(s, m.gb(2 + half), base, pairs)
            pe = end_unit(s, ins) if half else s.done(ins, "pe")
            s.wait(s.dve, pe, g0)
            t = s.done(s.dve.tensor_tensor(gate_keep[half], gate_keep[half], m.gb(2 + half), ALU.mult), "dve")
            s.last[("g", 2 + half)] = t
            s.wait(s.dve, t, d)
            y = m.big[:, cols]
            t = s.done(s.dve.tensor_tensor(y, y, gate_keep[half], ALU.add), "dve")
            s.last[keep_key[half]] = t
            return t

        gate_keep, keep_key = [m.rstd2, at], ["rstd2_read", "ss"]
        ctxs = []

        def gates_of(half):
            cols = bass.ds((i * 2 + half) * TILE, TILE)
            pe = full_tile(s, 0, m.nh, m.nl)
            d0 = scaled(s, gate_keep[half], m.gb(0), pe, ("g", 0), free=keep_key[half])
            pe = full_tile(s, 1, m.nh, m.nl)
            d1 = scaled(s, gate[half], m.gb(1), pe, ("g", 1), free=("sq", half))
            s.tables(SIGMOID)
            s.wait(s.act, d0)
            g0 = s.done(s.act.activation(gate_keep[half], gate_keep[half], ACT.Sigmoid), "act")
            s.wait(s.act, d1)
            g2 = s.done(s.act.activation(gate[half], gate[half], ACT.Sigmoid), "act")
            y = m.big[:, cols]
            s.wait(s.dve, g2)
            d = s.done(s.dve.tensor_tensor(y, y, gate[half], ALU.mult), "dve")
            s.last[("sq", half)] = d
            ctxs.append((g0, d, cols))

        d0 = softplus(0, scores(0))
        gates_of(0)
        x0 = suffix(0, d0)
        d1 = softplus(1, scores(1))
        values(0, x0)
        gates_of(1)
        x1 = suffix(1, d1)
        base = begin_unit(s)
        pooled(0, ctxs[0], base)
        s.last["merged"] = pooled(1, ctxs[1], base)
        mm = values(1, x1)
        s.last[("sb", 0)] = s.last[("sb", 1)] = s.last["vtok"] = mm
        _, lo = split(s, m.bigr[:, bass.ds(i * TILE + o_high, TILE)], m.bigr[:, bass.ds(i * TILE + o_low, TILE)],
                      m.ab(3), mm)
        s.last[("a", 3)] = lo
        s.last["sb_out"] = lo

    s.wait(s.dve, s.last["merged"])
    attend_banks_free(s)
    s.loop(4, body)
    s.last[("a", 1)] = s.last[("a", 2)] = s.last[("a", 0)]


def merge_branches(s):
    m = s.m
    o_high, o_low = 2 * KD * M + 8 * TILE, 2 * KD * M + 12 * TILE
    for j in range(0, KD, 2):
        gates = []
        for n in range(2):
            pe = full_tile(s, n, m.nh, m.nl)
            gt = m.sq[:, n * TILE:(n + 1) * TILE]
            d = scaled(s, gt, m.gb(n), pe, ("g", n), free=("sq", n))
            s.tables(SIGMOID)
            s.wait(s.act, d)
            gates.append(s.done(s.act.activation(gt, gt, ACT.Sigmoid), "act"))
        base = begin_unit(s)
        s.wait(s.pe, s.last["sb_out"])
        for n in range(2):
            gt = m.sq[:, n * TILE:(n + 1) * TILE]
            s.wait(s.pe, s.last.get(("g", 2 + n)))
            pairs = [(4 * n + kb, m.bigr[:, o_high + kb * TILE:o_high + (kb + 1) * TILE],
                      m.bigr[:, o_low + kb * TILE:o_low + (kb + 1) * TILE]) for kb in range(4)]
            ins = products(s, m.gb(2 + n), base, pairs)
            pe = end_unit(s, ins) if n else s.done(ins, "pe")
            y = m.big[:, (j + n) * TILE:(j + n + 1) * TILE]
            s.wait(s.dve, pe, gates[n], s.last["merged"])
            t = s.done(s.dve.tensor_tensor(gt, gt, m.gb(2 + n), ALU.mult), "dve")
            s.last[("g", 2 + n)] = t
            s.wait(s.dve, t)
            t = s.done(s.dve.tensor_tensor(y, y, gt, ALU.add), "dve")
            s.last[("sq", n)] = t
            s.last["merged"] = t
            sl = slice((j + n) * TILE, (j + n + 1) * TILE)
            _, lo = split(s, m.bigr[:, sl], m.bigr[:, (j + n + 8) * TILE:(j + n + 9) * TILE], y, t)
    s.last["n_read"] = pe
    s.wait(s.pe, lo)
    s.last["f"] = lo


def first_block(s):
    m = s.m
    memory_products(s)
    s.wait_value(s.act, m.s_x, 16, 0)
    s.wait_value(s.dve, m.s_x, 16, 0)
    rest = nothing
    for j in range(KD):
        before, rest = rest, operand_tile(s, "g_mix_pre", j, ())
        before()
    rest()
    wide_start(s)
    memory_values(s)
    memory_attention(s)
    cross_branch_out(s)
    stick_breaking(s)
    merge_branches(s)
    project_out(s, m.bigr[:, 0:8 * TILE], m.bigr[:, 8 * TILE:16 * TILE],
                lambda j, ps, pe, key: keep_branch(s, j, ps, pe, key))
    s.last["ff_read"] = s.last["n_read"]
    post_norm_add(s, "g_mix_post", "g_ffn_pre")

    def read_out(group, j, ps, pe, key):
        if group == 0:
            f = m.big[:, j * TILE:(j + 1) * TILE]
            s.wait(s.act, pe, s.last.get("f"))
            e = s.done(s.act.activation(f, ps, ACT.Copy), "act")
            s.last[key] = e
            s.last["f_acc"] = e
        else:
            keep_branch(s, j, ps, pe, key, acc=s.last["f_acc"])
    feed_forward(s, None, read_out, KD - 1)
    post_norm_add(s, "g_ffn_post", "g_mix2_0")


def lower_bounds(s):
    m = s.m
    lb, e, oml = m.small[:, 16:24], m.small[:, 24:32], m.small[:, 32:40]
    raw = m.col("hgrn_lb", 0, 8)
    d = s.done(s.dve.tensor_tensor(e, raw, raw, ALU.subtract), "dve")
    s.wait(s.act, d)
    x = s.done(s.act.activation(e, e, ACT.Exp), "act")
    s.wait(s.dve, x)
    d = s.done(s.dve.reciprocal(lb, e), "dve")
    s.wait(s.dve, d)
    d = s.done(s.dve.tensor_tensor(e, e, lb, ALU.mult), "dve")
    s.wait(s.dve, d)
    d = s.done(s.dve.tensor_tensor(lb, e, e, ALU.subtract), "dve")
    s.wait(s.dve, d)
    s.last["lb"] = s.done(s.dve.tensor_scalar(oml, lb, -1.0, 1.0, ALU.mult, ALU.add), "dve")


def recurrence(s):
    m = s.m
    t = lambda k: m.big[:, k * TILE:(k + 1) * TILE]
    key, qs, cum, sg, vt, vtok, diag, eg, kb_, tmp, o = (t(k) for k in range(11))
    xs = [t(11), t(12), t(17)]
    cross = m.big[:, 13 * TILE:13 * TILE + 768]
    qf, k0, q3 = t(15), m.big[:, 16 * TILE:16 * TILE + P], m.big[:, 16 * TILE + P:16 * TILE + 2 * P]
    blocks = lambda ap: ap.rearrange("p (c t) -> p c t", c=TB)
    s.wait(s.dve, s.last["lb"])
    s.last["diag"] = s.done(s.dve.memset(diag, 0.0), "dve")

    def project_fq():
        s.last["f_pe"] = full_tile(s, 0, m.nh, m.nl)
        s.last["q_pe"] = full_tile(s, 1, m.nh, m.nl)

    def next_fq():
        for bank, name in enumerate(("f_pe", "q_pe")):
            for mark in tile_quarters(s, bank, m.nh, m.nl):
                if mark is not None:
                    s.last[name] = mark
                yield

    def gate_chain(i, gate_before):
        d = scaled(s, tmp, m.gb(0), s.last["f_pe"], ("g", 0))
        s.tables(SIGMOID)
        s.wait(s.act, d)
        e = s.done(s.act.activation(tmp, tmp, ACT.Sigmoid), "act")
        dq = scaled(s, qs, m.gb(1), s.last["q_pe"], ("g", 1))
        s.wait(s.dve, e)
        d = s.done(s.dve.tensor_scalar(tmp, tmp, m.small[:, bass.ds(i + 32, 1)], m.small[:, bass.ds(i + 16, 1)],
                                       ALU.mult, ALU.add), "dve")
        s.wait(s.dve, d)
        k_in = s.done(s.dve.tensor_scalar(key, tmp, -1.0, 1.0, ALU.mult, ALU.add), "dve")
        d = s.done(s.dve.tensor_scalar(tmp, tmp, 2.0 ** -63, None, ALU.max), "dve")
        s.tables(SILU)
        s.wait(s.act, dq)
        e_q = s.done(s.act.activation(qs, qs, ACT.Silu), "act")
        if gate_before:
            s.wait(s.act, s.last["sg_in"])
            s.last["sg_ready"] = s.done(s.act.activation(sg, sg, ACT.Silu), "act")
        s.tables(LOGEXP)
        s.wait(s.act, d)
        e = s.done(s.act.activation(tmp, tmp, ACT.Ln), "act")
        s.wait(s.dve, e)
        c = s.done(s.dve.tensor_tensor_scan(cum, m.col("scan_keep", 0, S), tmp, 0.0, ALU.mult, ALU.add), "dve")
        return e_q, k_in, c

    def halves(ap, w):
        v = ap.rearrange("p (n a w) -> p n a w", a=2, w=w)
        return v[:, :, 0, :], v[:, :, 1, :]

    def distances(n):
        w, x = LEVELS[n], xs[n % 3]
        (g0, g1), (x0, x1) = halves(cum, w), halves(x, w)
        mid = g0[:, :, w - 1:w].broadcast_to([P, S // (2 * w), w])
        s.wait(s.dve, s.last.get(("xs", n % 3)))
        s.done(s.dve.tensor_tensor(x0, mid, g0, ALU.subtract), "dve")
        d = s.done(s.dve.tensor_tensor(x1, g1, mid, ALU.subtract), "dve")
        s.wait(s.act, d)
        return s.done(s.act.activation(x, x, ACT.Exp), "act")

    def factors(n, e):
        w, x = LEVELS[n], xs[n % 3]
        (x0, x1), (k0_, _), (_, q1) = halves(x, w), halves(key, w), halves(qs, w)
        s.wait(s.dve, e)
        s.done(s.dve.tensor_tensor(x0, x0, k0_, ALU.mult), "dve")
        return s.done(s.dve.tensor_tensor(x1, x1, q1, ALU.mult), "dve")

    def pair_scores(left, right, mark, bank):
        s.wait(s.pe, mark, s.last.get(("a", bank)))
        for c in range(TB):
            ins = s.pe.matmul(m.ab(bank, P, c * P), left[:, c * P:(c + 1) * P], right[:, c * P:(c + 1) * P],
                              start=c == 0, stop=c == TB - 1, skip_group_check=True)
        return s.done(ins, "pe")

    def keep_own(bank):
        mask = m.col("ident", 0, P).bitcast(U32).unsqueeze(1).broadcast_to([P, TB, P])
        d = s.done(s.dve.copy_predicated(blocks(diag), mask, blocks(m.ab(bank))), "dve")
        s.last[("a", bank)] = d
        s.last["diag_sum"] = d

    def keep_level(n, bank):
        w, pairs = LEVELS[n], P // (2 * LEVELS[n])
        mask = halves(m.col("levels", n * P, P), w)[1].bitcast(U32)
        if pairs == 1:
            mask = mask.broadcast_to([P, TB, w])
        else:
            mask = mask.unsqueeze(1).broadcast_to([P, TB, pairs, w])
        part = lambda ap: blocks(ap).rearrange("p c (n a w) -> p c n a w", a=2, w=w)[:, :, :, 1, :]
        d = s.done(s.dve.copy_predicated(part(diag), mask, part(m.ab(bank))), "dve")
        s.last[("a", bank)] = d
        s.last["diag_sum"] = d

    def carry_wait():
        s.dve.tensor_copy(m.small[:, 48:49], m.small[:, 16:17])

    def cross_factors(e_q, c):
        s.wait(s.act, c)
        e = s.done(s.act.activation(eg, cum, ACT.Exp), "act")
        last = blocks(cum)[:, :, P - 1:P].broadcast_to([P, TB, P])
        d = s.done(s.dve.tensor_tensor(blocks(kb_), last, blocks(cum), ALU.subtract), "dve")
        s.wait(s.act, d)
        e2 = s.done(s.act.activation(kb_, kb_, ACT.Exp), "act")
        s.wait(s.dve, e, e_q)
        s.done(s.dve.tensor_tensor(qf, qs, eg, ALU.mult), "dve")
        s.wait(s.dve, e2)
        d2 = s.done(s.dve.tensor_tensor(kb_, kb_, key, ALU.mult), "dve")
        s.wait(s.dve, d2)
        s.done(s.dve.tensor_scalar(k0, kb_[:, 0:P], eg[:, 2 * P - 1:2 * P], None, ALU.mult), "dve")
        return s.done(s.dve.tensor_scalar(q3, qf[:, 3 * P:4 * P], eg[:, 3 * P - 1:3 * P], None, ALU.mult), "dve")

    def cross_scores(d):
        s.wait(s.pe, d, s.last.get(("a", 1)), s.last.get(("a", 2)))
        for kk, qq, out, first in ((kb_[:, 0:P], qf[:, P:2 * P], 0, 1), (k0, qf[:, 2 * P:3 * P], 128, 0),
                                   (k0, q3, 256, 0), (kb_[:, P:2 * P], qf[:, 2 * P:3 * P], 384, 0),
                                   (kb_[:, P:2 * P], q3, 512, 1),
                                   (kb_[:, 2 * P:3 * P], qf[:, 3 * P:4 * P], 640, 0)):
            ins = s.pe.matmul(m.ab(1, P, out), kk, qq, start=bool(first), stop=False, skip_group_check=True)
        mm = s.done(ins, "pe")
        s.wait(s.act, mm)
        e = s.done(s.act.activation(cross, m.ab(1, 768), ACT.Copy), "act")
        s.last[("a", 1)] = s.last[("a", 2)] = e
        s.last["cross_ready"] = e

    def attend(i):
        s.wait(s.pe, s.last["vtok_ready"], s.last["diag_sum"], s.last["cross_ready"], s.last.get(("a", 3)))
        for c in range(TB):
            s.pe.matmul(m.ab(3, P, c * P), vtok[:, c * P:(c + 1) * P], diag[:, c * P:(c + 1) * P], start=c == 0,
                        stop=False, skip_group_check=True)
        for c, a, b in ((0, 0, 384), (1, 384, 640), (2, 640, 768)):
            ins = s.pe.matmul(m.ab(3, b - a, (c + 1) * P), vtok[:, c * P:(c + 1) * P], cross[:, a:b], start=False,
                              stop=c == 2, skip_group_check=True)
        mm = s.done(ins, "pe")
        s.last["vtok"] = s.last["attended"] = mm
        s.wait(s.act, mm, s.last.get("ss"), s.last.get("o"))
        q = s.done(s.act.activation(m.ss[:, :], m.ab(3), ACT.Square), "act")
        oc = s.done(s.act.activation(o, m.ab(3), ACT.Copy), "act")
        s.last[("a", 3)] = oc
        return q, oc

    def finish(i, q, oc):
        s.wait(s.act, s.last.get("rstd2_read"))
        r, mm2 = make_rstd(s, m.rstd2, P, A(s, 1), m.ss[:, :], q)
        s.last["ss"] = mm2
        s.wait(s.dve, r, oc)
        d = s.done(s.dve.scalar_tensor_tensor(out=o, in0=o, scalar=m.col("g_hgrn_out"), in1=m.rstd2,
                                              op0=ALU.mult, op1=ALU.mult), "dve")
        s.last["rstd2_read"] = d
        s.wait(s.dve, d, s.last["sg_ready"])
        d = s.done(s.dve.tensor_tensor(o, o, sg, ALU.mult), "dve")
        s.last["sg"] = d
        _, lo = split(s, m.bigr[:, bass.ds(i * TILE, TILE)], m.bigr[:, bass.ds(i * TILE + 8 * TILE, TILE)], o, d,
                      "ff_read")
        s.last["o_before"], s.last["o"] = s.last.get("o"), lo

    def head(i, before=None, after=next_fq):
        e_q, k_in, c = gate_chain(i, before is not None)
        s.wait(s.dve, c)
        exps = {0: distances(0), 1: distances(1)}
        pe = full_tile(s, 2, m.nh, m.nl)
        if before is not None:
            qo = attend(before)
        v = scaled(s, vt, m.gb(2), pe, ("g", 2), free="vt")
        f = factors(0, exps[0])
        exps[2] = distances(2)
        pe_gate = full_tile(s, 3, m.nh, m.nl)
        s.wait(s.pe, k_in)
        own = pair_scores(key, qs, e_q, 0)
        marks = pair_scores(xs[0], xs[0], f, 3)
        s.last[("xs", 0)] = marks
        f = factors(1, exps[1])
        if before is not None:
            finish(before, *qo)
        s.last["sg_in"] = scaled(s, sg, m.gb(3), pe_gate, ("g", 3), free="sg")
        s.last["vtok_ready"] = s.last["vt"] = to_tokens(s, vtok, vt, v, A(s, 2), "vtok")
        ahead = after()
        for _ in range(4):
            next(ahead)
        s.wait(s.dve, own, s.last.get("attended"), s.last["diag"])
        carry_wait()
        keep_own(0)
        crossed = cross_factors(e_q, c)
        for n in range(1, len(LEVELS)):
            if n > 1:
                f = factors(n, exps[n])
            s.wait(s.dve, marks, s.last["diag_sum"])
            if n + 2 < len(LEVELS):
                exps[n + 2] = distances(n + 2)
            else:
                carry_wait()
            keep_level(n - 1, 3 if n % 2 else 0)
            marks = pair_scores(xs[n % 3], xs[n % 3], f, 0 if n % 2 else 3)
            s.last[("xs", n % 3)] = marks
            if n < (5 if after is next_fq else 2):
                next(ahead)
            if n == 1:
                cross_scores(crossed)
        s.wait(s.dve, marks, s.last["diag_sum"])
        carry_wait()
        keep_level(len(LEVELS) - 1, 3)
        return ahead

    s.tables(LOGEXP)
    attend_banks_free(s)
    project_fq()
    head(0)
    s.loop(KD - 2, lambda i: head(i + 1, i))
    out = head(KD - 1, KD - 2, lambda: wide_tiles(s, m.bigr[:, 0:8 * TILE], m.bigr[:, 8 * TILE:16 * TILE],
                                                  lambda kb: s.last["o" if kb == KD - 1 else "o_before"]))
    s.last[("a", 2)] = s.last[("a", 1)]
    s.last["n_read"] = s.last["sg_in"]
    s.tables(SILU)
    s.wait(s.act, s.last["sg_in"])
    s.last["sg_ready"] = s.done(s.act.activation(sg, sg, ACT.Silu), "act")
    qo = attend(KD - 1)
    next(out)
    finish(KD - 1, *qo)
    next(out)
    next(out)


MLA_SIZE = 192


def rope_tables(s):
    m = s.m
    cos, sin = m.big[:, 18 * TILE:19 * TILE], m.big[:, 19 * TILE:20 * TILE]
    ang, k = m.big[:, 16 * TILE:17 * TILE], m.big[:, 17 * TILE:18 * TILE]
    pos = cos.bitcast(I32)
    R = slice(0, 64)
    two_pi = 2 * np.pi
    c1 = float(np.float32(6.28125))
    c2 = float(np.float32(np.round((two_pi - c1) * 2 ** 21) / 2 ** 21))
    c3 = float(np.float32(two_pi - c1 - c2))
    magic = 12582912.0
    s.wait_value(s.dve, m.s_pos, 16, 0)
    d = s.done(s.dve.tensor_copy(ang[R, :], pos[R, :]), "dve")
    s.wait(s.dve, d)
    d = s.done(s.dve.tensor_scalar(ang[R, :], ang[R, :], m.par[R, COL["inv_freq"]:COL["inv_freq"] + 1], None,
                                   ALU.mult), "dve")
    s.wait(s.dve, d)
    d = s.done(s.dve.tensor_scalar(k[R, :], ang[R, :], float(np.float32(1 / two_pi)), magic, ALU.mult, ALU.add), "dve")
    s.wait(s.dve, d)
    d = s.done(s.dve.tensor_scalar(k[R, :], k[R, :], magic, None, ALU.subtract), "dve")
    for c in (c1, c2, c3):
        s.wait(s.dve, d)
        d = s.done(s.dve.scalar_tensor_tensor(out=ang[R, :], in0=k[R, :], scalar=-c, in1=ang[R, :], op0=ALU.mult,
                                              op1=ALU.add), "dve")
    s.wait(s.dve, d)
    lim = 3.1415925
    d = s.done(s.dve.tensor_scalar(ang[R, :], ang[R, :], lim, -lim, ALU.min, ALU.max), "dve")
    s.tables(TRIG)
    s.wait(s.act, d, s.last.get("rstd2_read"))
    s.done(s.act.activation(sin[R, :], ang[R, :], ACT.Sin), "act")
    e = s.done(s.act.activation(cos[R, :], ang[R, :], ACT.Sin, scale=0.5), "act")
    s.wait(s.dve, e)
    d = s.done(s.dve.tensor_tensor(cos[R, :], cos[R, :], cos[R, :], ALU.mult), "dve")
    s.wait(s.dve, d)
    s.last["rope"] = s.done(s.dve.tensor_scalar(cos[R, :], cos[R, :], -2.0, 1.0, ALU.mult, ALU.add), "dve")


def latent_attention(s):
    m = s.m
    t = lambda k, n=1: m.big[:, k * TILE:(k + n) * TILE]
    cos, sin = t(18), t(19)
    lat_high, lat_low = m.bigr[:, 0:4 * TILE], m.bigr[:, 4 * TILE:8 * TILE]
    R = slice(0, 64)
    kr, krsq = t(0), t(1)

    def rotate(dst, src, mark, bank, tmp):
        s.wait(s.pe, mark, s.last.get(bank[1]))
        mm = s.done(s.pe.matmul(bank[0], m.col("swap", 0, P), src, start=True, stop=True), "pe")
        s.wait(s.dve, mark, s.last["rope"])
        d2 = s.done(s.dve.tensor_tensor(dst[R, :], src[R, :], cos[R, :], ALU.mult), "dve")
        s.wait(s.dve, mm)
        d = s.done(s.dve.tensor_tensor(tmp[R, :], bank[0][R, :], sin[R, :], ALU.mult), "dve")
        s.last[bank[1]] = d
        s.wait(s.dve, d, d2)
        return s.done(s.dve.tensor_tensor(dst[R, :], dst[R, :], tmp[R, :], ALU.add), "dve")

    for j in range(5):
        pe = full_tile(s, j % 4, m.nh, m.nl)
        dst = t(2 + j) if j < 4 else kr
        e = scaled(s, dst, m.gb(j % 4), pe, ("g", j % 4))
        if j < 4:
            add_square(s, dst, j, j % 2 == 0, (e,))()
            if j % 2:
                s.wait(s.act, s.last.get("latent_read"))
                r, _ = make_rstd(s, t(11), 256, A(s, 3))
                for k in (j - 1, j):
                    gain = m.col("g_qa" if j == 1 else "g_kva", k % 2)
                    s.wait(s.dve, r)
                    d = s.done(s.dve.scalar_tensor_tensor(out=t(2 + k), in0=t(2 + k), scalar=gain, in1=t(11),
                                                          op0=ALU.mult, op1=ALU.mult), "dve")
                    sl = slice(k * TILE, (k + 1) * TILE)
                    _, lo = split(s, lat_high[:, sl], lat_low[:, sl], t(2 + k), d, "ff_read")
                s.last["latent_read"] = d
    s.last["n_read"] = pe
    s.wait(s.act, e)
    sq = s.done(s.act.activation(krsq, kr, ACT.Square), "act")
    s.wait(s.dve, e, sq)
    d = s.done(s.dve.tensor_scalar(kr, kr, m.col("g_k", 1), None, ALU.mult), "dve")
    krot = t(2)
    s.wait(s.dve, lo)
    rot = rotate(krot, kr, d, A(s, 3), t(3))
    s.last["krot"] = rot
    s.wait(s.pe, lo, rot)

    qn, qr, kn, krn, vt, vtok, tmp, qrr = (t(k) for k in (3, 4, 5, 6, 7, 8, 9, 10))
    rq, rk = m.rstd[:, :], t(11)
    sqq, sqk = m.ss[:, :], m.sq[:, 0:TILE]
    sqt = m.sq[:, TILE:2 * TILE]
    probs = [m.big[:, 12 * TILE + o:12 * TILE + o + w] for o, w in ((0, 128), (128, 256), (384, 384), (768, 512))]
    pt = m.big[:, 15 * TILE:15 * TILE + ZW]
    scale = MLA_SIZE ** -0.5
    small = m.small

    def short_tile(bank, blk0):
        base = begin_unit(s)
        s.wait(s.pe, s.last.get(("g", bank)))
        pairs = [(kb, lat_high[:, (blk0 + kb) * TILE:(blk0 + kb + 1) * TILE],
                  lat_low[:, (blk0 + kb) * TILE:(blk0 + kb + 1) * TILE]) for kb in range(2)]
        return end_unit(s, products(s, m.gb(bank), base, pairs))

    def front_products():
        pes = [short_tile(b, 0 if b < 2 else 2) for b in range(4)]
        s.wait(s.act, pes[1], s.last.get("ss"), s.last.get(("sq", 1)))
        s.done(s.act.activation(sqq, m.gb(0), ACT.Square), "act")
        e = s.done(s.act.activation(sqt, m.gb(1), ACT.Square), "act")
        s.wait(s.dve, e)
        dq = s.done(s.dve.tensor_tensor(sqq, sqq, sqt, ALU.add), "dve")
        s.last[("sq", 1)] = dq
        s.wait(s.act, pes[2], s.last.get(("sq", 0)))
        e = s.done(s.act.activation(sqk, m.gb(2), ACT.Square), "act")
        s.wait(s.dve, e)
        dk = s.done(s.dve.tensor_tensor(sqk, sqk, krsq, ALU.add), "dve")
        s.wait(s.act, s.last.get("qk_read"))
        s.done(s.act.activation(qn, m.gb(0), ACT.Copy), "act")
        e1 = s.done(s.act.activation(qr, m.gb(1), ACT.Copy), "act")
        s.wait(s.dve, pes[3], s.last.get("qk_read"), s.last.get("vt"), e)
        e2 = s.done(s.dve.tensor_copy(kn, m.gb(2)), "dve")
        s.last["front_v"] = s.done(s.dve.tensor_copy(vt, m.gb(3)), "dve")
        for b, e in ((0, e1), (1, e1), (2, e2), (3, s.last["front_v"])):
            s.last[("g", b)] = e
        return dq, dk, e1

    def front_stats(dq, dk, e1):
        s.wait(s.act, s.last.get("rstd_read"))
        r, mm = make_rstd(s, rq, MLA_SIZE, G(s, 0), sqq, dq)
        s.last["ss"] = mm
        r2, mm = make_rstd(s, rk, MLA_SIZE, G(s, 1), sqk, dk)
        s.last[("sq", 0)] = mm
        return r, r2, e1

    def front_norms(r, r2, e1, between=nothing):
        s.wait(s.dve, r, e1)
        dr = s.done(s.dve.scalar_tensor_tensor(out=qr, in0=qr, scalar=m.col("g_q", 1), in1=rq, op0=ALU.mult,
                                               op1=ALU.mult), "dve")
        s.done(s.dve.scalar_tensor_tensor(out=qn, in0=qn, scalar=m.col("g_q", 0), in1=rq, op0=ALU.mult,
                                          op1=ALU.mult), "dve")
        s.wait(s.dve, r2, s.last["front_v"])
        s.last["front"] = s.done(s.dve.scalar_tensor_tensor(out=kn, in0=kn, scalar=m.col("g_k", 0), in1=rk,
                                                            op0=ALU.mult, op1=ALU.mult), "dve")
        between()
        rotate(qrr, qr, dr, G(s, 2), tmp)
        d = s.done(s.dve.tensor_tensor(krn[R, :], krot[R, :], rk[R, :], ALU.mult), "dve")
        s.last["rstd_read"] = d
        s.last["front_rotary"] = d

    def values_to_tokens():
        s.last["vtok_ready"] = to_tokens(s, vtok, vt, s.last["front_v"], G(s, 3), "vtok")
        s.last["vt"] = s.last["vtok_ready"]

    def scores():
        s.wait(s.pe, s.last["front"])
        marks = []
        for qb in range(TB):
            s.wait(s.pe, s.last.get(("a", qb)))
            n = (qb + 1) * P
            s.pe.matmul(m.ab(qb, n), qn[:, qb * P:n], kn[:, 0:n], start=True, stop=False, skip_group_check=True)
        s.wait(s.pe, s.last["front_rotary"])
        for qb in range(TB):
            n = (qb + 1) * P
            qsl = slice(qb * P, n)
            s.pe.matmul(m.ab(qb, n), qrr[R, qsl], krn[R, 0:n], start=False, stop=False, skip_group_check=True)
            ins = s.pe.matmul(m.ab(qb, P, qb * P), m.col("ident", 0, P), m.col("mla_mask", 0, P), start=False,
                              stop=True, skip_group_check=True)
            marks.append(s.done(ins, "pe"))
        s.last["qk_read"] = marks[-1]
        return marks

    def softmax(marks):
        mx, nb, sm = (small[:, o:o + TB] for o in (0, 4, 8))
        s.wait(s.dve, s.last.get("mla_small"))
        maxima = []
        for qb in range(TB):
            s.wait(s.dve, marks[qb])
            d = s.done(s.dve.tensor_reduce(mx[:, qb:qb + 1], m.ab(qb, (qb + 1) * P), AX_X, ALU.max), "dve")
            s.wait(s.dve, d)
            maxima.append(s.done(s.dve.tensor_scalar(nb[:, qb:qb + 1], mx[:, qb:qb + 1], -scale, None, ALU.mult), "dve"))
        exps = []
        for qb in range(TB):
            s.wait(s.act, maxima[qb], s.last.get("prob"))
            e = s.done(s.act.activation(probs[qb], m.ab(qb, (qb + 1) * P), ACT.Exp, bias=nb[:, qb:qb + 1],
                                        scale=scale, accum_out=sm[:, qb:qb + 1]), "act")
            s.last[("a", qb)] = e
            exps.append(e)
        s.wait(s.dve, exps[-1])
        d = s.done(s.dve.reciprocal(sm, sm), "dve")
        s.wait(s.dve, d)
        for qb in range(TB):
            d = s.done(s.dve.tensor_scalar(probs[qb], probs[qb], sm[:, qb:qb + 1], None, ALU.mult), "dve")
        s.last["mla_small"] = d
        return d

    def transpose_probs(d):
        s.wait(s.pe, d, s.last.get(("a", 0)), s.last.get(("a", 1)), s.last.get(("a", 2)))
        for qb in range(TB):
            for kb in range(qb + 1):
                ins = s.pe.transpose(m.ab(0, P, ZOFF[kb] + (qb - kb) * P), probs[qb][:, kb * P:(kb + 1) * P],
                                     m.col("ident", 0, P))
        tr = s.done(ins, "pe")
        s.last["prob"] = tr
        s.wait(s.act, tr, s.last.get("pt"))
        e = s.done(s.act.activation(pt, m.ab(0, ZW), ACT.Copy), "act")
        s.last[("a", 0)] = s.last[("a", 1)] = s.last[("a", 2)] = e
        return e

    def attend(e):
        s.wait(s.pe, e, s.last["vtok_ready"], s.last.get(("a", 3)))
        for kb in range(TB):
            w = S - kb * P
            ins = s.pe.matmul(m.ab(3, w, kb * P), vtok[:, kb * P:(kb + 1) * P], pt[:, ZOFF[kb]:ZOFF[kb] + w],
                              start=kb == 0, stop=kb == 3, skip_group_check=True)
        mm = s.done(ins, "pe")
        s.last["pt"] = s.last["vtok"] = mm
        return mm

    def keep_output(i, mm):
        _, lo = split(s, m.bigr[:, bass.ds(i * TILE + 8 * TILE, TILE)], m.bigr[:, bass.ds(i * TILE + 16 * TILE, TILE)],
                      m.ab(3), mm)
        s.last[("a", 3)] = lo
        s.last["mla_out"] = lo

    front_norms(*front_stats(*front_products()))
    values_to_tokens()

    def body(i):
        d = softmax(scores())
        f = front_products()
        e = transpose_probs(d)
        f = front_stats(*f)
        mm = attend(e)
        front_norms(*f, lambda: keep_output(i, mm))
        values_to_tokens()
    s.loop(KD - 2, body)
    body(KD - 2)
    d = softmax(scores())
    out = wide_tiles(s, m.bigr[:, 8 * TILE:16 * TILE], m.bigr[:, 16 * TILE:24 * TILE], lambda kb: s.last["mla_out"])
    for _ in range(4):
        next(out)
    e = transpose_probs(d)
    next(out)
    next(out)
    mm = attend(e)
    next(out)
    keep_output(KD - 1, mm)
    next(out)


def second_block(s):
    m = s.m
    wide_start(s)
    lower_bounds(s)
    recurrence(s)
    project_out(s, m.bigr[:, 0:8 * TILE], m.bigr[:, 8 * TILE:16 * TILE],
                lambda j, ps, pe, key: residual_add(s, j, ps, pe, key, "g_ffn2_0"))
    s.last["ff_read"] = s.last["n_read"]
    conv_feed_forward(s, 0, "g_mix2_1", lambda: rope_tables(s))
    wide_start(s)
    latent_attention(s)
    project_out(s, m.bigr[:, 8 * TILE:16 * TILE], m.bigr[:, 16 * TILE:24 * TILE],
                lambda j, ps, pe, key: residual_add(s, j, ps, pe, key, "g_ffn2_1"))
    s.last["ff_read"] = s.last["n_read"]
    conv_feed_forward(s, 1)


def conv_feed_forward(s, layer, gain=None, during=None):
    def read_out(group, j, ps, pe, key):
        if group and gain:
            residual_add(s, j, ps, pe, key, gain)
            return
        h = s.m.h[:, j * TILE:(j + 1) * TILE]
        s.wait(s.dve, pe, s.last.get("h"))
        a = s.done(s.dve.tensor_tensor(h, h, ps, ALU.add), "dve")
        s.last[key] = a
        if group:
            s.outputs.append(a)
        elif j == KD - 1:
            s.last["h"] = a
    feed_forward(s, layer, read_out, KD - 3, during)


def weight_units(w):
    full, short = [], []

    def tile(mat, c, width=P):
        x = mat[:, c:c + width].reshape(-1, P, width).transpose(1, 0, 2)
        return np.pad(x, ((0, 0), (0, 0), (0, P - width))) if width < P else x

    def ffn(w_in, w_down):
        t0 = 0
        for n in GROUPS:
            for j in range(t0, t0 + n):
                full.extend((tile(w_in, j * P), tile(w_in, FF + j * P)))
            for j in range(t0, t0 + n):
                full.append(w_down[j * P:(j + 1) * P].reshape(P, KD, P))
            t0 += n

    w_in, gates = w["w_in"][0], 2304
    full += [tile(w["w_mem_kv"][0], j * P) for j in range(4)]
    full += [tile(w_in, 2048 + j * P) for j in range(2)]
    full += [tile(w_in, j * P) for j in range(4)]
    for u in range(2):
        full.append(np.concatenate([tile(w["w_x_o"][0], (4 * u + k) * P) for k in range(4)], axis=1))
    for i in range(4):
        full += [tile(w_in, 512 * (n + 1) + i * P) for n in range(3)]
        for j in (2 * i, 2 * i + 1):
            full += [tile(w_in, gates + b * D + j * P) for b in (0, 2)]
        full.append(np.concatenate([tile(w["w_pool_o"][0], j * P) for j in (2 * i, 2 * i + 1)], axis=1))
    for j in range(0, KD, 2):
        full += [tile(w_in, gates + D + k * P) for k in (j, j + 1)]
        full.append(np.concatenate([tile(w["w_sb_o"][0], k * P) for k in (j, j + 1)], axis=1))
    full += [tile(w["w_out"][0], j * P) for j in range(KD)]
    ffn(w["w_ffn_in"][0], w["w_ffn_out"][0])
    hgrn = w["hgrn_w_in_2"][0]
    for h in range(KD):
        if h == 0:
            full += [tile(hgrn, part * D) for part in (1, 0)]
        full += [tile(hgrn, part * D + h * P) for part in (2, 3)]
        if h < KD - 1:
            full += [tile(hgrn, part * D + (h + 1) * P) for part in (1, 0)]
    full += [tile(w["hgrn_w_out_2"][0], j * P) for j in range(KD)]
    ffn(w["ffn_w_up_2"][0], w["ffn_w_down_2"][0])
    mla = w["mla_w_in_2"][0]
    full += [tile(mla, j * P) for j in range(4)] + [tile(mla, 4 * P, 64)]
    before = len(full)
    for h in range(KD):
        q, kv = w["mla_w_q_up_2"][0], w["mla_w_kv_up_2"][0]
        short += [tile(q, h * MLA_SIZE), tile(q, h * MLA_SIZE + P, 64), tile(kv, h * 2 * P), tile(kv, h * 2 * P + P)]
    full += [tile(w["mla_w_out_2"][0], j * P) for j in range(KD)]
    ffn(w["ffn_w_up_2"][1], w["ffn_w_down_2"][1])
    return full, short, before


def packed(parts, width):
    out = np.empty((len(parts), P, width), np.float32)
    for n, x in enumerate(parts):
        out[n] = x.reshape(P, width)
    return out


def parameters(w):
    par = np.zeros((P, NCOL), np.float32)

    def vec(name, v):
        v = np.asarray(v).reshape(-1)
        n = -(-v.size // P)
        par[:, COL[name]:COL[name] + n] = np.pad(v, (0, n * P - v.size)).reshape(n, P).T

    for name, key in (("g_mix_pre", "norm_mix_pre"), ("g_mem", "norm_mem"), ("pool_scale", "pool_scale"),
                      ("g_mix_post", "norm_mix_post"), ("g_ffn_pre", "norm_ffn_pre"), ("g_ffn_post", "norm_ffn_post"),
                      ("hgrn_lb", "hgrn_lower_bounds_2"), ("g_hgrn_out", "hgrn_out_norm_2"),
                      ("g_qa", "mla_q_a_norm_2"), ("g_kva", "mla_kv_a_norm_2"), ("g_q", "mla_q_norm_2"),
                      ("g_k", "mla_k_norm_2")):
        vec(name, w[key])
    for n in range(2):
        vec(f"g_mix2_{n}", w["norm_mix_2"][n])
        vec(f"g_ffn2_{n}", w["norm_ffn_2"][n])
        vec(f"conv_w{n}", w["ffn_conv_w_2"][n])
        vec(f"conv_b{n}", w["ffn_conv_b_2"][n])

    def mat(name, x):
        par[:x.shape[0], COL[name]:COL[name] + x.shape[1]] = x

    mat("w_mix", w["w_pool_mix"][0].transpose(1, 0, 2).reshape(P, 4 * P))
    r, c = np.arange(P)[:, None], np.arange(P)[None, :]
    mat("ident", r == c)
    mat("ones", np.ones((P, P)))
    mat("neg_tri", -(r >= c).astype(np.float32))
    mat("neg_ones", -np.ones((P, P)))
    mat("sb_mask", np.where(r >= c, NEG, 0.0))
    mat("mla_mask", np.where(c > r, NEG, 0.0))
    levels = [(r // (2 * w) == c // (2 * w)) & (r // w % 2 == 0) & (c // w % 2 == 1) for w in LEVELS]
    mat("levels", np.concatenate(levels, axis=1))
    mat("scan_keep", np.broadcast_to(np.arange(S) % P != 0, (P, S)))
    t = np.arange(16)
    edge = np.concatenate([win / np.minimum(t + 1, win) for win in (2, 4, 8, 16)])
    mat("pool_edge", np.broadcast_to(edge, (P, 64)))
    mat("inv_freq", np.concatenate([INV_FREQ, INV_FREQ])[:, None])
    k, o = np.arange(64)[:, None], np.arange(64)[None, :]
    mat("swap", np.where(k == o - 32, 1.0, 0.0) - np.where(k == o + 32, 1.0, 0.0))
    mat("eps", np.full((P, 1), EPS))
    mat("one", np.ones((P, 1)))
    return par


def feature_tiles(x):
    return np.ascontiguousarray(x.T.reshape(KD, P, x.shape[0]).transpose(1, 0, 2).reshape(P, -1))


N_SHORT = 4 * KD


def run_schedule(nc, ctx, mem, active, real, n_full, before):
    s = Schedule(nc, ctx, mem, active, real)
    s.n_units = n_full + N_SHORT
    s.short = lambda u: before <= u < before + N_SHORT
    s.outputs = []
    for name, owner in (("pe", "pe"), ("act", "act"), ("dve", "dve"), ("hi", "act"), ("use", "pe")):
        if owner == active:
            real.sem_inc(mem.sems[name], Count.START)
    first_block(s)
    second_block(s)
    assert s.unit_a == s.n_units, (s.unit_a, s.n_units)
    return s


def build(nc, n_full, before):
    dram = lambda name, shape, dt=F32, kind="ExternalInput": nc.dram_tensor(name, shape, dt, kind=kind).ap()
    x = dram("x_tiles", (P, KD * TILE))
    memory = dram("memory_tiles", (P, KD * M))
    par = dram("params", (P, NCOL))
    pos = dram("positions", (64, S), I32)
    w_full = dram("weights_full", (n_full, P, UNIT))
    w_short = dram("weights_short", (N_SHORT, P, UNIT_S))
    out = dram("out_tiles", (P, KD * TILE), kind="ExternalOutput")

    with ExitStack() as ctx:
        m = Memory(nc, ctx)
        block = ctx.enter_context(nc.Block())
        outputs = run_schedule(nc, ctx, m, "none", None, n_full, before).outputs
        segments = ((0, before, w_full, 0, UNIT), (before, N_SHORT, w_short, 0, UNIT_S),
                    (before + N_SHORT, n_full - before, w_full, before, UNIT))

        def over_units(eng, body):
            for first, n, src, index, width in segments:
                peel = SLOTS + WIDE if first == 0 else 0
                rounds = (n - peel) // SLOTS
                for k in range(peel):
                    body(first + k, 0, src, index + k, width)
                with eng.Fori(0, rounds) as i:
                    for k in range(SLOTS):
                        body(first + peel + k, i * SLOTS, src, index + peel + k, width)
                for k in range(peel + rounds * SLOTS, n):
                    body(first + k, 0, src, index + k, width)

        @block.sync
        def _(sp):
            sp.dma_start(m.par[:, 0:FIRST_COLS], par[:, 0:FIRST_COLS]).then_inc(m.s_gains, 16)
            sp.dma_start(m.big[:, 4 * TILE:8 * TILE], memory).then_inc(m.s_mem, 16)

            def load(u, ahead, src, index, width):
                j = u % SLOTS
                if u >= SLOTS:
                    sp.wait_ge(m.s_lo, ahead + (u - SLOTS + 1))
                sp.dma_start(m.raw[:, j * UNIT:j * UNIT + width], src[bass.ds(ahead + index, 1)]
                             .rearrange("a p n -> (a p) n")).then_inc(m.s_raw[j], 16)
                if u == WIDE - 1:
                    sp.dma_start(m.h[:, :], x).then_inc(m.s_x, 16)
                if u == SLOTS + WIDE - 1:
                    sp.dma_start(m.par[:, FIRST_COLS:NCOL], par[:, FIRST_COLS:NCOL]).then_inc(m.s_par, 16)
                    sp.dma_start(m.big[0:64, 18 * TILE:19 * TILE].bitcast(I32), pos).then_inc(m.s_pos, 16)
            over_units(sp, load)
            for j, mark in enumerate(outputs):
                sp.wait_ge(mark.count.sem, mark.a)
                sl = slice(j * TILE, (j + 1) * TILE)
                sp.dma_start(out[:, sl], m.h[:, sl]).then_inc(m.s_out, 16)
            sp.wait_ge(m.s_out, 16 * KD)

        @block.gpsimd
        def _(pool):
            def low(u, ahead, src, index, width):
                j = u % SLOTS
                pool.wait_ge(m.sems["hi"], ahead + (Count.START + u + 1))
                sl = slice(j * UNIT, j * UNIT + width)
                pool.tensor_tensor(m.wl[:, sl], m.raw[:, sl], m.wh[:, sl].bitcast(F32), ALU.subtract)\
                    .then_inc(m.s_lo, 1)
            over_units(pool, low)

        @block.scalar
        def _(act):
            run_schedule(nc, ctx, m, "act", act, n_full, before)

        @block.vector
        def _(dve):
            run_schedule(nc, ctx, m, "dve", dve, n_full, before)

        @block.tensor
        def _(pe):
            run_schedule(nc, ctx, m, "pe", pe, n_full, before)


def kernel(**inputs):
    import concourse.bacc as bacc
    from concourse.bass_utils import run_bass_kernel_spmd

    w = {k: np.asarray(v) for k, v in inputs.items()}
    full, short, before = weight_units(w)
    arrays = {
        "x_tiles": feature_tiles(w["x"][0]),
        "memory_tiles": feature_tiles(w["mem"][0]),
        "params": parameters(w),
        "positions": np.ascontiguousarray(np.broadcast_to(w["positions_2"], (64, S))),
        "weights_full": packed(full, UNIT),
        "weights_short": packed(short, UNIT_S),
    }
    nc = bacc.Bacc("TRN2", target_bir_lowering=False, num_devices=1)
    build(nc, len(full), before)
    r = run_bass_kernel_spmd(nc, [arrays], core_ids=[0])
    y = r.results[0]["out_tiles"].reshape(P, KD, S)
    return np.ascontiguousarray(y.transpose(2, 1, 0).reshape(1, S, D))
```
